# Optimizing a Trainium2 kernel written in Bass

```python
import jax, jax.numpy as jnp
from jax import lax
import numpy as np
import math

D_MODEL = 2048
BATCH = 1
SEQ = 256
DEPTH = 1

MLA_HEADS = 8
MLA_Q_RANK = 512
MLA_KV_RANK = 512
MLA_NOPE_DIM = 128
MLA_ROPE_DIM = 64
MLA_V_DIM = 128
MLA_WIDTH = MLA_HEADS * MLA_V_DIM
MLA_IN = MLA_Q_RANK + MLA_KV_RANK + MLA_ROPE_DIM
ROPE_THETA = 10000.0
Q_BLOCK = 128

RWKV_HEAD = 64
RWKV_HEADS = 16
RWKV_WIDTH = RWKV_HEADS * RWKV_HEAD
DECAY_RANK = 96
ICLR_RANK = 96
RWKV_SIZES = [RWKV_WIDTH, RWKV_WIDTH, RWKV_WIDTH, DECAY_RANK, DECAY_RANK, ICLR_RANK, ICLR_RANK]
RWKV_IN = sum(RWKV_SIZES)
GN_EPS = 64e-5
NORM_EPS = 1e-6

IN_SIZES = [MLA_IN, RWKV_IN, MLA_WIDTH, RWKV_WIDTH, D_MODEL, D_MODEL]
D_IN = sum(IN_SIZES)


def _offsets(sizes):
    return [int(o) for o in np.cumsum(sizes)[:-1]]

def rms_norm(x, g, eps=NORM_EPS):
    xf = x.astype(jnp.float32)
    y = xf * lax.rsqrt(jnp.mean(xf * xf, axis=-1, keepdims=True) + eps)
    return (y * g.astype(jnp.float32)).astype(x.dtype)

def apply_rotary(t, cos, sin):
    tf = t.astype(jnp.float32)
    t1, t2 = jnp.split(tf, 2, axis=-1)
    return jnp.concatenate([t1 * cos - t2 * sin, t1 * sin + t2 * cos], axis=-1).astype(t.dtype)

def centred_shift(p):
    pad = jnp.pad(p, ((0, 0), (1, 1), (0, 0)))
    return 0.5 * (pad[:, :-2] + pad[:, 2:])

def mla_attention(q_nope, q_rope, k_nope, k_rope, v):
    B, S, H, _ = q_nope.shape
    nb = S // Q_BLOCK
    scale = (MLA_NOPE_DIM + MLA_ROPE_DIM) ** -0.5
    qn = q_nope.reshape(B, nb, Q_BLOCK, H, MLA_NOPE_DIM).transpose(1, 0, 2, 3, 4)
    qr = q_rope.reshape(B, nb, Q_BLOCK, H, MLA_ROPE_DIM).transpose(1, 0, 2, 3, 4)

    def block(args):
        qn_b, qr_b = args
        s = (jnp.einsum('bqhd,bkhd->bhqk', qn_b, k_nope, preferred_element_type=jnp.float32)
             + jnp.einsum('bqhr,bkr->bhqk', qr_b, k_rope, preferred_element_type=jnp.float32))
        p = jax.nn.softmax(s * scale, axis=-1)
        return jnp.einsum('bhqk,bkhd->bqhd', p.astype(v.dtype), v)

    o = lax.map(block, (qn, qr))
    return o.transpose(1, 0, 2, 3, 4).reshape(B, S, H * MLA_V_DIM)

def rwkv7_bidir_scan(r, w_f, w_b, k_f, k_b, v, kk, a_f, a_b):
    B, S, H, N = r.shape

    def tm(fwd, bwd):
        return jnp.stack([fwd, bwd[:, ::-1]], axis=0).transpose(2, 0, 1, 3, 4)

    xs = (tm(r, r), tm(w_f, w_b), tm(k_f, k_b), tm(v, v), tm(-kk, -kk), tm(kk * a_f, kk * a_b))

    def step(st, inp):
        r_t, w_t, k_t, v_t, a_t, b_t = inp
        sa = jnp.einsum('dbhij,dbhj->dbhi', st, a_t)
        st = st * w_t[..., None, :] + sa[..., None] * b_t[..., None, :] + v_t[..., None] * k_t[..., None, :]
        y = jnp.einsum('dbhij,dbhj->dbhi', st, r_t)
        return st, y

    s0 = jnp.zeros((2, B, H, N, N), jnp.float32)
    _, ys = lax.scan(step, s0, xs)
    y = ys[:, 0] + ys[::-1, 1]
    return y.transpose(1, 0, 2, 3)

def first_inputs(seed: int = 0) -> dict:
    key = jax.random.key(seed)
    ks = jax.random.split(key, 32)
    f32 = jnp.float32
    nrm = lambda k, shape, s: jax.random.normal(k, shape, f32) * s
    gain = lambda k, n: 1.0 + nrm(k, (n,), 0.02)
    return {
        "x": nrm(ks[0], (BATCH, SEQ, D_MODEL), 1.0),
        "g_pre": gain(ks[1], D_MODEL),
        "w_in": nrm(ks[2], (D_MODEL, D_IN), D_MODEL ** -0.5),
        "mla_q_norm": gain(ks[3], MLA_Q_RANK),
        "mla_wq_b": nrm(ks[4], (MLA_Q_RANK, MLA_HEADS * (MLA_NOPE_DIM + MLA_ROPE_DIM)), MLA_Q_RANK ** -0.5),
        "mla_kv_norm": gain(ks[5], MLA_KV_RANK),
        "mla_wkv_b": nrm(ks[6], (MLA_KV_RANK, MLA_HEADS * (MLA_NOPE_DIM + MLA_V_DIM)), MLA_KV_RANK ** -0.5),
        "rwkv_mu": jax.random.uniform(ks[7], (RWKV_IN,), f32),
        "rwkv_w0_f": nrm(ks[8], (RWKV_WIDTH,), 0.5),
        "rwkv_w2_f": nrm(ks[9], (DECAY_RANK, RWKV_WIDTH), 0.5 * DECAY_RANK ** -0.5),
        "rwkv_w0_b": nrm(ks[10], (RWKV_WIDTH,), 0.5),
        "rwkv_w2_b": nrm(ks[11], (DECAY_RANK, RWKV_WIDTH), 0.5 * DECAY_RANK ** -0.5),
        "rwkv_a0_f": nrm(ks[12], (RWKV_WIDTH,), 0.1),
        "rwkv_a2_f": nrm(ks[13], (ICLR_RANK, RWKV_WIDTH), 0.5 * ICLR_RANK ** -0.5),
        "rwkv_a0_b": nrm(ks[14], (RWKV_WIDTH,), 0.1),
        "rwkv_a2_b": nrm(ks[15], (ICLR_RANK, RWKV_WIDTH), 0.5 * ICLR_RANK ** -0.5),
        "rwkv_k_k": 0.85 + nrm(ks[16], (RWKV_WIDTH,), 0.02),
        "rwkv_k_a": gain(ks[17], RWKV_WIDTH),
        "rwkv_r_k": nrm(ks[18], (RWKV_HEADS, RWKV_HEAD), 0.1),
        "rwkv_gn_g": gain(ks[19], RWKV_WIDTH),
        "rwkv_gn_b": nrm(ks[20], (RWKV_WIDTH,), 0.01),
        "w_br_mla": nrm(ks[21], (MLA_WIDTH, D_MODEL), MLA_WIDTH ** -0.5),
        "w_br_rwkv": nrm(ks[22], (RWKV_WIDTH, D_MODEL), RWKV_WIDTH ** -0.5),
        "w_out": nrm(ks[23], (D_MODEL, D_MODEL), D_MODEL ** -0.5),
        "g_post": gain(ks[24], D_MODEL),
    }

def first_block(x, g_pre, w_in, mla_q_norm, mla_wq_b, mla_kv_norm, mla_wkv_b, rwkv_mu,
              rwkv_w0_f, rwkv_w2_f, rwkv_w0_b, rwkv_w2_b, rwkv_a0_f, rwkv_a2_f, rwkv_a0_b,
              rwkv_a2_b, rwkv_k_k, rwkv_k_a, rwkv_r_k, rwkv_gn_g, rwkv_gn_b, w_br_mla,
              w_br_rwkv, w_out, g_post):
    f32 = jnp.float32
    B, S, _ = x.shape
    pos = jnp.arange(S, dtype=f32)
    inv_freq = jnp.power(ROPE_THETA, -jnp.arange(0, MLA_ROPE_DIM, 2, dtype=f32) / MLA_ROPE_DIM)
    ang = pos[:, None] * inv_freq[None, :]
    cos, sin = jnp.cos(ang), jnp.sin(ang)

    for _layer in range(DEPTH):
        h = rms_norm(x, g_pre)
        proj = h @ w_in
        mla_in, rwkv_in, z_mla, z_rwkv, gate_mla, gate_rwkv = jnp.split(proj, _offsets(IN_SIZES), axis=-1)

        q_a, kv_a, k_rope = jnp.split(mla_in, _offsets([MLA_Q_RANK, MLA_KV_RANK, MLA_ROPE_DIM]), axis=-1)
        q = (rms_norm(q_a, mla_q_norm) @ mla_wq_b).reshape(B, S, MLA_HEADS, MLA_NOPE_DIM + MLA_ROPE_DIM)
        kv = (rms_norm(kv_a, mla_kv_norm) @ mla_wkv_b).reshape(B, S, MLA_HEADS, MLA_NOPE_DIM + MLA_V_DIM)
        q_nope, q_rope = q[..., :MLA_NOPE_DIM], q[..., MLA_NOPE_DIM:]
        k_nope, v_mla = kv[..., :MLA_NOPE_DIM], kv[..., MLA_NOPE_DIM:]
        q_rope = apply_rotary(q_rope, cos[:, None, :], sin[:, None, :])
        k_rope = apply_rotary(k_rope, cos, sin)
        y_mla = mla_attention(q_nope, q_rope, k_nope, k_rope, v_mla)

        rin = rwkv_in.astype(f32)
        rin = rin + rwkv_mu * (centred_shift(rin) - rin)
        r, k, v, wd_f, wd_b, ad_f, ad_b = jnp.split(rin, _offsets(RWKV_SIZES), axis=-1)

        def decay(w0, wd, w2):
            z = w0 + jnp.tanh(wd) @ w2
            return jnp.exp(-jnp.exp(-jax.nn.softplus(-z) - 0.5))

        w_f = decay(rwkv_w0_f.astype(f32), wd_f, rwkv_w2_f.astype(f32))
        w_b = decay(rwkv_w0_b.astype(f32), wd_b, rwkv_w2_b.astype(f32))
        a_f = jax.nn.sigmoid(rwkv_a0_f.astype(f32) + ad_f @ rwkv_a2_f.astype(f32))
        a_b = jax.nn.sigmoid(rwkv_a0_b.astype(f32) + ad_b @ rwkv_a2_b.astype(f32))

        hd = lambda t: t.reshape(B, S, RWKV_HEADS, RWKV_HEAD)
        kk = hd(k * rwkv_k_k.astype(f32))
        kk = kk / jnp.maximum(jnp.linalg.norm(kk, axis=-1, keepdims=True), 1e-12)
        k_a = rwkv_k_a.astype(f32)
        k_f = k * (1.0 + (a_f - 1.0) * k_a)
        k_b = k * (1.0 + (a_b - 1.0) * k_a)
        r_h, v_h, k_fh, k_bh = hd(r), hd(v), hd(k_f), hd(k_b)
        y = rwkv7_bidir_scan(r_h, hd(w_f), hd(w_b), k_fh, k_bh, v_h, kk, hd(a_f), hd(a_b))
        mu = jnp.mean(y, axis=-1, keepdims=True)
        var = jnp.mean(jnp.square(y - mu), axis=-1, keepdims=True)
        yn = ((y - mu) * lax.rsqrt(var + GN_EPS)).reshape(B, S, RWKV_WIDTH)
        yn = yn * rwkv_gn_g.astype(f32) + rwkv_gn_b.astype(f32)
        bonus = jnp.sum(r_h * (k_fh + k_bh) * rwkv_r_k.astype(f32), axis=-1, keepdims=True) * v_h
        y_rwkv = (yn + bonus.reshape(B, S, RWKV_WIDTH)).astype(x.dtype)

        u_mla = (y_mla * jax.nn.silu(z_mla)) @ w_br_mla
        u_rwkv = (y_rwkv * jax.nn.silu(z_rwkv)) @ w_br_rwkv
        merged = jax.nn.sigmoid(gate_mla) * u_mla + jax.nn.sigmoid(gate_rwkv) * u_rwkv
        out = merged @ w_out
        x = (x + rms_norm(out, g_post)).astype(x.dtype)
    return x


_first_inputs = first_inputs


def first_inputs(seed=0):
    import zlib

    import numpy as np

    out = dict(_first_inputs(seed))
    spreads = {}
    factors = {'mla_q_norm': 8.0,
     'mla_kv_norm': 8.0,
     'rwkv_k_k': 64.0,
     'rwkv_k_a': 3.275,
     'rwkv_gn_g': 25.426,
     'rwkv_gn_b': 53.148,
     'g_post': 11.765,
     'rwkv_w2_f': 3.013,
     'rwkv_w2_b': 3.004}
    for name, (base, spread) in spreads.items():
        noise = np.random.default_rng([zlib.crc32(name.encode()), seed]).standard_normal(out[name].shape)
        drawn = base * np.exp(spread * noise) if base else spread * noise
        out[name] = __import__('jax').numpy.asarray(drawn.astype(out[name].dtype))
    for name, factor in factors.items():
        out[name] = (out[name] * factor).astype(out[name].dtype)
    return out


_narrow_inputs = first_inputs


def first_inputs(seed=0):

    out = dict(_narrow_inputs(seed))
    wider = {'rwkv_k_k': 11.61, 'rwkv_r_k': 4.62, 'rwkv_gn_g': 3.35, 'rwkv_gn_b': 3.31, 'g_post': 3.21}
    for name, times in wider.items():
        mean = out[name].mean()
        out[name] = (mean + times * (out[name] - mean)).astype(out[name].dtype)
    return out


PLE_DIM = 256
CONV_WIDTH = 31
HEAD_DIM = D_MODEL // 16
CONV_HEADS = 8
POOL_GROUPS = 4
FOURIER_HEADS = 4
CONV_DIM = CONV_HEADS * HEAD_DIM
POOL_DIM = POOL_GROUPS * HEAD_DIM
FOURIER_DIM = FOURIER_HEADS * HEAD_DIM
MIX_DIM = CONV_DIM + POOL_DIM + FOURIER_DIM
IN_DIM = 2 * CONV_DIM + POOL_DIM + FOURIER_DIM
POOL_WINDOWS = (2, 4, 8, 16)
D_FF = -(-8 * D_MODEL // (3 * 256)) * 256
ALPHA = (2 * DEPTH) ** 0.25
BETA = (8 * DEPTH) ** -0.25
LN_EPS = 1e-5


def layer_norm(x, g, b):
    xf = x.astype(jnp.float32)
    mu = jnp.mean(xf, axis=-1, keepdims=True)
    var = jnp.mean(jnp.square(xf - mu), axis=-1, keepdims=True)
    y = (xf - mu) * lax.rsqrt(var + LN_EPS) * g.astype(jnp.float32) + b.astype(jnp.float32)
    return y.astype(x.dtype)

def conformer_conv(val, gate, w_dw, b_dw, ln_g, ln_b):
    u = val * jax.nn.sigmoid(gate)
    y = lax.conv_general_dilated(
        u, w_dw[:, None, :].astype(u.dtype), window_strides=(1,),
        padding=[(CONV_WIDTH // 2, CONV_WIDTH // 2)],
        dimension_numbers=("NWC", "WIO", "NWC"),
        feature_group_count=CONV_DIM) + b_dw
    return jax.nn.silu(layer_norm(y, ln_g, ln_b))

def multiscale_pool(u, w_pool, b_pool, scale):
    B, S, _ = u.shape
    ug = u.reshape(B, S, POOL_GROUPS, HEAD_DIM).astype(jnp.float32)
    t = jnp.arange(S)
    outs = []
    for g, k in enumerate(POOL_WINDOWS):
        xg = ug[:, :, g, :]
        cs = jnp.concatenate([jnp.zeros((B, 1, HEAD_DIM), jnp.float32),
                              jnp.cumsum(xg, axis=1)], axis=1)
        lo = jnp.clip(t - k // 2, 0, S)
        hi = jnp.clip(t + k // 2, 0, S)
        cnt = (hi - lo).astype(jnp.float32)[None, :, None]
        mean = (jnp.take(cs, hi, axis=1) - jnp.take(cs, lo, axis=1)) / cnt
        outs.append(mean - xg)
    pooled = jnp.stack(outs, axis=2).astype(u.dtype)
    y = jnp.einsum("bsgc,gcd->bsgd", pooled, w_pool) + b_pool
    y = y * scale.reshape(POOL_GROUPS, HEAD_DIM)
    return y.reshape(B, S, POOL_DIM)

def fourier_mix(u, w_f, b_f):
    B, S, _ = u.shape
    uh = u.reshape(B, S, FOURIER_HEADS, HEAD_DIM).astype(jnp.float32)
    zf = jnp.fft.fftn(uh, axes=(1, 3), norm="ortho").real.astype(u.dtype)
    y = jnp.einsum("bshc,hcd->bshd", zf, w_f) + b_f
    return y.reshape(B, S, FOURIER_DIM)

def second_inputs(seed: int = 0) -> dict:
    key = jax.random.key(seed)
    ks = jax.random.split(key, 32)
    f32 = jnp.float32

    def nrm(k, shape, scale):
        return jax.random.normal(k, shape, f32) * scale

    L = DEPTH
    return {
        "x": nrm(ks[0], (BATCH, SEQ, D_MODEL), 1.0),
        "p": nrm(ks[1], (DEPTH, BATCH, SEQ, PLE_DIM), 1.0),
        "w_in": nrm(ks[2], (L, D_MODEL, IN_DIM), D_MODEL ** -0.5),
        "b_in": nrm(ks[3], (L, IN_DIM), 0.02),
        "w_dw": nrm(ks[4], (L, CONV_WIDTH, CONV_DIM), CONV_WIDTH ** -0.5),
        "b_dw": nrm(ks[5], (L, CONV_DIM), 0.02),
        "conv_ln_g": 1.0 + nrm(ks[6], (L, CONV_DIM), 0.02),
        "conv_ln_b": nrm(ks[7], (L, CONV_DIM), 0.02),
        "w_pool": nrm(ks[8], (L, POOL_GROUPS, HEAD_DIM, HEAD_DIM), HEAD_DIM ** -0.5),
        "b_pool": nrm(ks[9], (L, POOL_GROUPS, HEAD_DIM), 0.02),
        "pool_scale": 1.0 + nrm(ks[10], (L, POOL_DIM), 0.02),
        "w_fourier": nrm(ks[11], (L, FOURIER_HEADS, HEAD_DIM, HEAD_DIM), HEAD_DIM ** -0.5),
        "b_fourier": nrm(ks[12], (L, FOURIER_HEADS, HEAD_DIM), 0.02),
        "w_out": nrm(ks[13], (L, MIX_DIM, D_MODEL), BETA * MIX_DIM ** -0.5),
        "b_out": nrm(ks[14], (L, D_MODEL), 0.02),
        "ln1_g": 1.0 + nrm(ks[15], (L, D_MODEL), 0.02),
        "ln1_b": nrm(ks[16], (L, D_MODEL), 0.02),
        "w_gate": nrm(ks[17], (L, D_MODEL, D_FF), D_MODEL ** -0.5),
        "w_up": nrm(ks[18], (L, D_MODEL, D_FF), D_MODEL ** -0.5),
        "w_down": nrm(ks[19], (L, D_FF, D_MODEL), BETA * D_FF ** -0.5),
        "w_ple": nrm(ks[20], (L, PLE_DIM, D_MODEL), BETA * PLE_DIM ** -0.5),
        "w_ple_gate": nrm(ks[21], (L, D_MODEL, D_MODEL), D_MODEL ** -0.5),
        "ln2_g": 1.0 + nrm(ks[22], (L, D_MODEL), 0.02),
        "ln2_b": nrm(ks[23], (L, D_MODEL), 0.02),
    }

def second_block(x, p, w_in, b_in, w_dw, b_dw, conv_ln_g, conv_ln_b, w_pool, b_pool,
              pool_scale, w_fourier, b_fourier, w_out, b_out, ln1_g, ln1_b,
              w_gate, w_up, w_down, w_ple, w_ple_gate, ln2_g, ln2_b):
    s1 = CONV_DIM
    s2 = 2 * CONV_DIM
    s3 = 2 * CONV_DIM + POOL_DIM
    for i in range(DEPTH):
        z = jnp.einsum("bsd,de->bse", x, w_in[i]) + b_in[i]
        y_conv = conformer_conv(z[..., :s1], z[..., s1:s2], w_dw[i], b_dw[i],
                                conv_ln_g[i], conv_ln_b[i])
        y_pool = multiscale_pool(z[..., s2:s3], w_pool[i], b_pool[i], pool_scale[i])
        y_four = fourier_mix(z[..., s3:], w_fourier[i], b_fourier[i])
        mixed = jnp.concatenate([y_conv, y_pool, y_four], axis=-1)
        mix_out = jnp.einsum("bsm,md->bsd", mixed, w_out[i]) + b_out[i]
        x = layer_norm(ALPHA * x + mix_out, ln1_g[i], ln1_b[i])
        hid = jax.nn.silu(jnp.einsum("bsd,df->bsf", x, w_gate[i])) * \
            jnp.einsum("bsd,df->bsf", x, w_up[i])
        ffn = jnp.einsum("bsf,fd->bsd", hid, w_down[i])
        ple = jax.nn.sigmoid(jnp.einsum("bsd,de->bse", x, w_ple_gate[i])) * \
            jnp.einsum("bsq,qd->bsd", p[i], w_ple[i])
        x = layer_norm(ALPHA * x + ffn + ple, ln2_g[i], ln2_b[i])
    return x


_first_inputs_2 = second_inputs


def second_inputs(seed=0):
    import zlib

    import numpy as np

    out = dict(_first_inputs_2(seed))
    spreads = {}
    factors = {'b_in': 8.0,
     'b_dw': 6.972,
     'conv_ln_g': 8.0,
     'conv_ln_b': 8.0,
     'b_pool': 8.0,
     'pool_scale': 8.0,
     'b_fourier': 8.0,
     'b_out': 3.458,
     'ln1_g': 2.71,
     'ln1_b': 2.864,
     'ln2_g': 2.83,
     'ln2_b': 2.879}
    for name, (base, spread) in spreads.items():
        noise = np.random.default_rng([zlib.crc32(name.encode()), seed]).standard_normal(out[name].shape)
        drawn = base * np.exp(spread * noise) if base else spread * noise
        out[name] = __import__('jax').numpy.asarray(drawn.astype(out[name].dtype))
    for name, factor in factors.items():
        out[name] = (out[name] * factor).astype(out[name].dtype)
    return out


_narrow_inputs_2 = second_inputs


def second_inputs(seed=0):

    out = dict(_narrow_inputs_2(seed))
    wider = {'conv_ln_g': 3.5,
     'conv_ln_b': 3.79,
     'pool_scale': 4.03,
     'b_fourier': 3.73,
     'ln2_g': 3.17,
     'ln2_b': 3.18}
    for name, times in wider.items():
        mean = out[name].mean()
        out[name] = (mean + times * (out[name] - mean)).astype(out[name].dtype)
    return out


HEAD_DIM_3 = 128
N_HEADS_SB = (D_MODEL // HEAD_DIM_3) // 2
N_HEADS_DSA = (D_MODEL // HEAD_DIM_3) - N_HEADS_SB
SB_WIDTH = N_HEADS_SB * HEAD_DIM_3
DSA_WIDTH = N_HEADS_DSA * HEAD_DIM_3
IDX_HEADS = 16
IDX_DIM = 64
TOPK_MAX = 256
ROPE_THETA_3 = 500000.0
ROPE_FRACTION = 4
D_FF_3 = 5504
CONV_WIDTH_3 = 3
EPS = 1e-6
NEG_BIG = -1e30

COL_SIZES = (
    SB_WIDTH, SB_WIDTH, SB_WIDTH,
    DSA_WIDTH, HEAD_DIM_3, HEAD_DIM_3,
    IDX_HEADS * IDX_DIM, IDX_DIM,
    IDX_HEADS,
)
IN_COLS = sum(COL_SIZES)
SPLIT_POINTS = tuple(int(v) for v in np.cumsum(COL_SIZES)[:-1])


def rmsnorm(x, g):
    x32 = x.astype(jnp.float32)
    y = x32 * lax.rsqrt(jnp.mean(x32 * x32, axis=-1, keepdims=True) + EPS)
    return (y * g.astype(jnp.float32)).astype(x.dtype)

def rope_partial(x, pos):
    d = x.shape[-1]
    rd = d // ROPE_FRACTION
    half = rd // 2
    inv_freq = ROPE_THETA_3 ** (-jnp.arange(half, dtype=jnp.float32) / half)
    ang = pos.astype(jnp.float32)[..., None] * inv_freq
    cos = jnp.cos(ang)[:, :, None, :]
    sin = jnp.sin(ang)[:, :, None, :]
    x32 = x.astype(jnp.float32)
    x1, x2, rest = x32[..., :half], x32[..., half:rd], x32[..., rd:]
    out = jnp.concatenate([x1 * cos - x2 * sin, x2 * cos + x1 * sin, rest], axis=-1)
    return out.astype(x.dtype)

def stick_breaking_attention(q, k, v):
    S = q.shape[1]
    scale = q.shape[-1] ** -0.5
    outs = []
    for start in range(0, S, Q_BLOCK):
        end = start + Q_BLOCK
        qb, kb, vb = q[:, start:end], k[:, :end], v[:, :end]
        z = jnp.einsum('bqhd,bkhd->bhqk', qb, kb).astype(jnp.float32) * scale
        t_idx = start + jnp.arange(Q_BLOCK)[:, None]
        s_idx = jnp.arange(end)[None, :]
        strict = s_idx < t_idx
        log_1m = jnp.where(strict, jax.nn.log_sigmoid(-z), 0.0)
        key_axis = log_1m.ndim - 1
        suffix = lax.cumsum(log_1m, axis=key_axis, reverse=True) - log_1m
        w = jnp.where(strict, jnp.exp(jax.nn.log_sigmoid(z) + suffix), 0.0)
        outs.append(jnp.einsum('bhqk,bkhd->bqhd', w.astype(vb.dtype), vb))
    return jnp.concatenate(outs, axis=1)

def dsa_attention(q, k, v, q_idx, k_idx, w_idx):
    S = q.shape[1]
    topk = min(TOPK_MAX, S // 4)
    scale = q.shape[-1] ** -0.5
    gather = jax.vmap(lambda arr, idx: arr[idx])
    outs = []
    for start in range(0, S, Q_BLOCK):
        end = start + Q_BLOCK
        L = max(end, topk)
        rel = jax.nn.relu(jnp.einsum('bqhd,bkd->bqhk', q_idx[:, start:end],
                                     k_idx[:, :L]).astype(jnp.float32))
        score = jnp.einsum('bqh,bqhk->bqk', w_idx[:, start:end].astype(jnp.float32), rel)
        t_idx = start + jnp.arange(Q_BLOCK)[:, None]
        causal = jnp.arange(L)[None, :] <= t_idx
        score = jnp.where(causal, score, NEG_BIG)
        _, sel = lax.top_k(score, topk)
        valid = sel <= t_idx[None]
        k_sel = gather(k, sel)
        v_sel = gather(v, sel)
        logits = jnp.einsum('bqhd,bqkd->bhqk', q[:, start:end], k_sel).astype(jnp.float32) * scale
        logits = jnp.where(valid[:, None], logits, NEG_BIG)
        p = jax.nn.softmax(logits, axis=-1)
        outs.append(jnp.einsum('bhqk,bqkd->bqhd', p.astype(v_sel.dtype), v_sel))
    return jnp.concatenate(outs, axis=1)

def conv_ffn(h, w_up, conv_w, conv_b, w_down):
    S = h.shape[1]
    u = h @ w_up
    up = jnp.pad(u, ((0, 0), (CONV_WIDTH_3 - 1, 0), (0, 0)))
    uc = conv_b
    for i in range(CONV_WIDTH_3):
        uc = uc + up[:, i:i + S] * conv_w[i]
    gate, val = jnp.split(uc, 2, axis=-1)
    return (jax.nn.silu(gate) * val) @ w_down

def third_inputs(seed: int = 0) -> dict:
    key = jax.random.key(seed)
    ks = jax.random.split(key, 20)
    D = D_MODEL
    f32 = jnp.float32
    nrm = lambda k, shape, s: jax.random.normal(k, shape, f32) * s
    x = nrm(ks[0], (BATCH, SEQ, D), 1.0)
    c = nrm(ks[1], (BATCH, D), 1.0)
    offset = jax.random.randint(ks[2], (BATCH, 1), 0, 1024, dtype=jnp.int32)
    positions = (offset + jnp.arange(SEQ, dtype=jnp.int32)[None, :]).astype(jnp.int32)
    return {
        "x": x,
        "c": c,
        "positions": positions,
        "w_ada": nrm(ks[3], (DEPTH, D, 6 * D), 0.5 * D ** -0.5),
        "b_ada": nrm(ks[4], (DEPTH, 6 * D), 0.01),
        "norm1_g": 1.0 + nrm(ks[5], (DEPTH, D), 0.01),
        "w_in": nrm(ks[6], (DEPTH, D, IN_COLS), D ** -0.5),
        "sb_norm_g": 1.0 + nrm(ks[7], (DEPTH, SB_WIDTH), 0.01),
        "dsa_norm_g": 1.0 + nrm(ks[8], (DEPTH, DSA_WIDTH), 0.01),
        "w_out": nrm(ks[9], (DEPTH, SB_WIDTH + DSA_WIDTH, D), (SB_WIDTH + DSA_WIDTH) ** -0.5),
        "norm2_g": 1.0 + nrm(ks[10], (DEPTH, D), 0.01),
        "w_up": nrm(ks[11], (DEPTH, D, 2 * D_FF_3), D ** -0.5),
        "conv_w": nrm(ks[12], (DEPTH, CONV_WIDTH_3, 2 * D_FF_3), CONV_WIDTH_3 ** -0.5),
        "conv_b": nrm(ks[13], (DEPTH, 2 * D_FF_3), 0.01),
        "w_down": nrm(ks[14], (DEPTH, D_FF_3, D), D_FF_3 ** -0.5),
        "final_norm_g": 1.0 + nrm(ks[15], (D,), 0.01),
    }

def third_block(x, c, positions, w_ada, b_ada, norm1_g, w_in, sb_norm_g, dsa_norm_g,
              w_out, norm2_g, w_up, conv_w, conv_b, w_down, final_norm_g):
    B, S, D = x.shape
    idx_scale = (IDX_HEADS ** -0.5) * (IDX_DIM ** -0.5)
    for l in range(DEPTH):
        mod = jax.nn.silu(c) @ w_ada[l] + b_ada[l]
        sh1, sc1, g1, sh2, sc2, g2 = jnp.split(mod[:, None, :], 6, axis=-1)

        h = rmsnorm(x, norm1_g[l]) * (1.0 + sc1) + sh1
        proj = h @ w_in[l]
        q_sb, k_sb, v_sb, q_ds, k_ds, v_ds, q_ix, k_ix, w_ix = jnp.split(proj, SPLIT_POINTS, axis=-1)

        q_sb = q_sb.reshape(B, S, N_HEADS_SB, HEAD_DIM_3)
        k_sb = k_sb.reshape(B, S, N_HEADS_SB, HEAD_DIM_3)
        v_sb = v_sb.reshape(B, S, N_HEADS_SB, HEAD_DIM_3)
        o_sb = stick_breaking_attention(q_sb, k_sb, v_sb).reshape(B, S, SB_WIDTH)

        q_ds = rope_partial(q_ds.reshape(B, S, N_HEADS_DSA, HEAD_DIM_3), positions)
        k_ds = rope_partial(k_ds[:, :, None, :], positions)[:, :, 0, :]
        q_ix = rope_partial(q_ix.reshape(B, S, IDX_HEADS, IDX_DIM), positions)
        k_ix = rope_partial(k_ix[:, :, None, :], positions)[:, :, 0, :]
        o_ds = dsa_attention(q_ds, k_ds, v_ds, q_ix, k_ix, w_ix * idx_scale).reshape(B, S, DSA_WIDTH)

        merged = jnp.concatenate([rmsnorm(o_sb, sb_norm_g[l]), rmsnorm(o_ds, dsa_norm_g[l])], axis=-1)
        x = x + g1 * (merged @ w_out[l])

        h2 = rmsnorm(x, norm2_g[l]) * (1.0 + sc2) + sh2
        x = x + g2 * conv_ffn(h2, w_up[l], conv_w[l], conv_b[l], w_down[l])
    return rmsnorm(x, final_norm_g)


_first_inputs_3 = third_inputs


def third_inputs(seed=0):
    import zlib

    import numpy as np

    out = dict(_first_inputs_3(seed))
    spreads = {}
    factors = {'b_ada': 2.994,
     'norm1_g': 4.323,
     'sb_norm_g': 8.0,
     'dsa_norm_g': 8.0,
     'norm2_g': 8.0,
     'conv_b': 8.0,
     'final_norm_g': 5.493}
    for name, (base, spread) in spreads.items():
        noise = np.random.default_rng([zlib.crc32(name.encode()), seed]).standard_normal(out[name].shape)
        drawn = base * np.exp(spread * noise) if base else spread * noise
        out[name] = __import__('jax').numpy.asarray(drawn.astype(out[name].dtype))
    for name, factor in factors.items():
        out[name] = (out[name] * factor).astype(out[name].dtype)
    return out


_narrow_inputs_3 = third_inputs


def third_inputs(seed=0):

    out = dict(_narrow_inputs_3(seed))
    wider = {'sb_norm_g': 6.91,
     'dsa_norm_g': 7.26,
     'norm2_g': 4.89,
     'conv_b': 4.75,
     'final_norm_g': 6.25}
    for name, times in wider.items():
        mean = out[name].mean()
        out[name] = (mean + times * (out[name] - mean)).astype(out[name].dtype)
    return out


def setup_inputs(seed=0):
    out = dict(first_inputs(seed))
    for name, value in second_inputs(seed + 1).items():
        if name != "x":
            out[name + "_2"] = value
    for name, value in third_inputs(seed + 2).items():
        if name != "x":
            out[name + "_3"] = value
    return out


def reference(
    x, g_pre, w_in, mla_q_norm, mla_wq_b, mla_kv_norm, mla_wkv_b, rwkv_mu, rwkv_w0_f, rwkv_w2_f,
    rwkv_w0_b, rwkv_w2_b, rwkv_a0_f, rwkv_a2_f, rwkv_a0_b, rwkv_a2_b, rwkv_k_k, rwkv_k_a,
    rwkv_r_k, rwkv_gn_g, rwkv_gn_b, w_br_mla, w_br_rwkv, w_out, g_post, p_2, w_in_2, b_in_2,
    w_dw_2, b_dw_2, conv_ln_g_2, conv_ln_b_2, w_pool_2, b_pool_2, pool_scale_2, w_fourier_2,
    b_fourier_2, w_out_2, b_out_2, ln1_g_2, ln1_b_2, w_gate_2, w_up_2, w_down_2, w_ple_2,
    w_ple_gate_2, ln2_g_2, ln2_b_2, c_3, positions_3, w_ada_3, b_ada_3, norm1_g_3, w_in_3,
    sb_norm_g_3, dsa_norm_g_3, w_out_3, norm2_g_3, w_up_3, conv_w_3, conv_b_3, w_down_3,
    final_norm_g_3,
):
    x = first_block(
        x, g_pre, w_in, mla_q_norm, mla_wq_b, mla_kv_norm, mla_wkv_b, rwkv_mu, rwkv_w0_f,
        rwkv_w2_f, rwkv_w0_b, rwkv_w2_b, rwkv_a0_f, rwkv_a2_f, rwkv_a0_b, rwkv_a2_b, rwkv_k_k,
        rwkv_k_a, rwkv_r_k, rwkv_gn_g, rwkv_gn_b, w_br_mla, w_br_rwkv, w_out, g_post,
    )
    x = second_block(
        x, p_2, w_in_2, b_in_2, w_dw_2, b_dw_2, conv_ln_g_2, conv_ln_b_2, w_pool_2, b_pool_2,
        pool_scale_2, w_fourier_2, b_fourier_2, w_out_2, b_out_2, ln1_g_2, ln1_b_2, w_gate_2,
        w_up_2, w_down_2, w_ple_2, w_ple_gate_2, ln2_g_2, ln2_b_2,
    )
    return third_block(
        x, c_3, positions_3, w_ada_3, b_ada_3, norm1_g_3, w_in_3, sb_norm_g_3, dsa_norm_g_3,
        w_out_3, norm2_g_3, w_up_3, conv_w_3, conv_b_3, w_down_3, final_norm_g_3,
    )


_drawn_inputs = setup_inputs


def setup_inputs(seed=0):
    import zlib

    import numpy as np

    out = dict(_drawn_inputs(seed))
    spreads = {}
    factors = {}
    for name, (base, spread) in spreads.items():
        noise = np.random.default_rng([zlib.crc32(name.encode()), seed]).standard_normal(out[name].shape)
        drawn = base * np.exp(spread * noise) if base else spread * noise
        out[name] = __import__('jax').numpy.asarray(drawn.astype(out[name].dtype))
    for name, factor in factors.items():
        out[name] = (out[name] * factor).astype(out[name].dtype)
    return out
```

```python
from contextlib import ExitStack

import numpy as np
import concourse.bass as bass
from concourse import mybir

F32 = mybir.dt.float32
F32R = mybir.dt.float32r
I32 = mybir.dt.int32
ACT = mybir.ActivationFunctionType
ALU = mybir.AluOpType
AX = mybir.AxisListType

P = 128
T = 256
D = 2048
DC = D // P
COLS = 512
KPS = 4
SLOT = KPS * COLS
RING = 4
WORK = 39600
HEADS = 8
RANK = 512
NOPE, ROPE = 128, 64
WIDTH = 1024
LORA = 96
CH = 64
PAIRS = 8
KAPPA = float(np.exp(-0.5))
EPS = 1e-6
EPS_GN = 64e-5
EPS_LN = 1e-5
ALPHA = 2.0 ** 0.25
TAPS = 31
POOL_WINDOWS = (2, 4, 8, 16)
FF2 = 5632
FF3 = 5504
FF3_CHUNKS = 44
IDX_HEADS, IDX_DIM = 16, 64
TOPK = 64
NEG = -1e30
TAKEN = -3e38
TRI = 384

STREAM = [
    ("qa", 4, 1), ("kva", 4, 1), ("kr", 1, 1), ("lora", 4, 1), ("rkv", 4, 6), ("z", 4, 2),
    ("q_nope", 1, 2), ("q_rope", 1, 1), ("k_nope", 1, 2), ("v_mla", 1, 2), ("z2", 4, 2),
    ("gates", 4, 8), ("br_mla", 2, 4), ("br_rwkv", 2, 4), ("w_out", 4, 4),
    ("conv_in", 4, 4), ("pool_in", 4, 1), ("four_in", 4, 1), ("poolmat", 1, 1), ("seqmat", 1, 1), ("four_w", 1, 1),
    ("w_out2", 4, 4), ("ffn2", 4, 22), ("down2", 16, 4),
    ("misc", 4, 1), ("q_ix", 4, 2), ("qk_sb", 4, 4), ("v_q", 4, 4),
    ("w_out3", 4, 4), ("ffn3", 4, 22), ("down3", 11, 4),
]
FIRST = {}
_n = 0
for _name, _per, _groups in STREAM:
    FIRST[_name] = (_n, _per)
    _n += _per * _groups
SLOTS = _n


def slot0(stage, j=0):
    return FIRST[stage][0] + FIRST[stage][1] * j


def used(stage, j=0):
    return slot0(stage, j + 1)


ADA_GROUPS = 6 * D // COLS
ADA_RUNS = [(RING, 8), (96, 16)]
assert sum(n for _, n in ADA_RUNS) == ADA_GROUPS
ADA_RING = 2
ADA_SUMS = 4

SPLIT = [("ffn2", "down2"), ("ffn3", "down3")]
SPLIT_SLOTS = []
for _first, _last in SPLIT:
    _stage = next(s for s in STREAM if s[0] == _last)
    SPLIT_SLOTS += range(slot0(_first), slot0(_last, _stage[2]))
SPLIT_AT = {n: k for k, n in enumerate(SPLIT_SLOTS)}


PARAMS = [[
    ("g_pre", 16), ("q_norm", 4), ("kv_norm", 4), ("mu_lora", 4), ("mu_rkv", 24), ("pair", 8 * PAIRS),
    ("k_k", 8), ("gn_g", 8), ("gn_b", 8), ("g_post", 16), ("c", 16),
], [
    ("b_in", 24), ("taps", 8 * TAPS), ("b_dw", 8), ("cln_g", 8), ("cln_b", 8), ("b_pool", 4), ("s_pool", 4),
    ("b_four", 4), ("b_out", 16), ("ln1_g", 16), ("ln1_b", 16), ("ln2_g", 16), ("ln2_b", 16),
    ("b_ada", 96),
], [
    ("n1_g", 16), ("sb_g", 8), ("ds_g", 8), ("n2_g", 16),
    ("conv_w", 3 * 2 * FF3_CHUNKS), ("conv_b", 2 * FF3_CHUNKS), ("fin_g", 16),
]]
PAR = {}
for _block in PARAMS:
    _n = 0
    for _name, _w in _block:
        PAR[_name] = _n
        _n += _w
NPAR = [sum(w for _, w in b) for b in PARAMS]
PAIR_PARAMS = 8

C_ALL = [("ident", P), ("ones", P), ("eps", 4)]
C_1 = [("bones", P), ("swap", P), ("cos", T), ("sin", T), ("reset", T), ("lvl", 2 * 6 * P), ("strict", 2 * CH),
       ("incl", 2 * CH), ("lmask", 2 * P)]
C_3 = [("swap128", P), ("swap64", P), ("tri", P), ("sp_mask", TRI), ("sp_min", TRI), ("causal", TRI), ("cneg", TRI),
       ("freq", 8), ("e0", P)]


def offsets(items, at=0):
    out = {}
    for name, w in items:
        out[name] = at
        at += w
    return out, at


OFF_ALL, N_ALL = offsets(C_ALL)
OFF_1, N_1 = offsets(C_1, N_ALL)
OFF_3, N_3 = offsets(C_3, N_ALL)
N_CONST = max(N_1, N_3)


class Tally:

    def __init__(self, eng):
        self.eng, self.n, self.i, self.step = eng, {}, None, {}

    def value(self, sem):
        v = self.n.get(sem.name, 0)
        return v + self.i * self.step[sem.name] if self.step.get(sem.name) else v

    def give(self, ins, sem, by=1):
        self.n[sem.name] = self.n.get(sem.name, 0) + by
        ins.then_inc(sem, by)

    def wait(self, sem, more=0):
        self.n[sem.name] = self.n.get(sem.name, 0) + more
        self.eng.wait_ge(sem, self.value(sem))

    def enter(self, i, step):
        self.i, self.step, self.was = i, {s.name: k for s, k in step.items()}, dict(self.n)

    def leave(self, trips):
        for name, n in self.n.items():
            moved = n - self.was.get(name, 0)
            assert moved == self.step.get(name, 0), (name, moved, self.step.get(name, 0))
            self.n[name] = n + (trips - 1) * moved
        self.i, self.step = None, {}


GROUPS = [
    ("qa", 1, (0,)), ("kva", 1, (1,)), ("kr", 1, (0,)), ("lora", 1, (1,)), ("rkv", 6, (0, 1)), ("z", 2, (0, 1)),
    ("q_nope", 2, (0, 1)), ("q_rope", 1, (0,)), ("k_nope", 2, (1, 0)), ("v_mla", 2, (1, 0)), ("z2", 2, (1, 0)),
    ("gates", 8, (0,)), ("br_mla", 4, (0, 1)), ("br_rwkv", 4, (0, 1)), ("w_out", 4, (0, 1)),
    ("conv_in", 4, (0, 1)), ("pool_in", 1, (0,)), ("four_in", 1, (1,)), ("w_out2", 4, (0, 1)),
    ("ffn2", 22, (0, 1)), ("down2", 4, (0,)), ("ple_gate", 4, (1,)),
    ("misc", 1, (0,)), ("q_ix", 2, (1, 0)), ("qk_sb", 4, (1, 0)), ("v_q", 4, (1, 0)),
    ("w_out3", 4, (1, 0)), ("ffn3", 22, (0, 1)), ("down3", 4, (0, 1)),
]
MAGIC = 1.5 * 2.0 ** 23
TWO_PI = (6.28125, 1.9350051879882812e-03, 3.019916050561733e-07)
PI_BELOW = 3.1415925
V_STEPS = 21
PAIR = {}
_n = [0, 0]
for _name, _groups, _cycle in GROUPS:
    for _j in range(_groups):
        _p = _cycle[_j % len(_cycle)]
        _n[_p] += 1
        PAIR[_name, _j] = (_p, _n[_p])


def build_program(nc, a):
    ctx = ExitStack()

    def sb(name, shape, dt=F32):
        return ctx.enter_context(nc.sbuf_tensor(name, shape, dt))

    sems = {}

    def S(name):
        if name not in sems:
            sems[name] = ctx.enter_context(nc.semaphore(name))
        return sems[name]

    ring_at = -(-nc.sbuf_base // 32) * 32
    ring = sb("ring", [P, RING, SLOT])
    ring_parts = nc.alloc_sbuf_tensor_at("ring_parts", [P, RING, SLOT], F32R, offset=ring_at)
    CON = sb("con", [P, N_CONST])
    PR = sb("par", [P, max(NPAR)])
    X = sb("resid", [P, DC, T])
    MOD = sb("mod", [P, 96])
    CS = sb("cs", [P, 16])
    RED = sb("red", [P, 2, T])
    STD = sb("std", [P, 2, T])
    work_at = -(-nc.sbuf_base // 32) * 32
    W = sb("work", [P, WORK])
    PS = ctx.enter_context(nc.psum_tensor("ps", [P, 8, 512], F32))

    def w(at, *shape):
        n = int(np.prod(shape))
        v = W[:, at:at + n]
        names = "abcde"[:len(shape)]
        if len(shape) == 1:
            return v
        return v.rearrange(f"p ({' '.join(names)}) -> p {' '.join(names)}", **{k: s for k, s in zip(names[1:], shape[1:])})

    def own(name, at, *shape, dt=F32R):
        return nc.alloc_sbuf_tensor_at(name, [P, *shape], dt, offset=work_at + 4 * at)[:]

    def con(name, n, at=0):
        off = {**OFF_ALL, **OFF_1, **OFF_3}[name]
        return CON[:, off + at:off + at + n]

    def par(name, k=0, n=1):
        return PR[:, PAR[name] + k:PAR[name] + k + n]

    def rows(x, n):
        return x.unsqueeze(1).broadcast_to([x.shape[0], n, x.shape[1]])

    ident, ones = con("ident", P), con("ones", P)
    loaded = [S(f"w_loaded{k}") for k in range(RING)]
    w_used = S("w_used")
    read_out = [S("read_out0"), S("read_out1")]

    H = w(0, DC, T)
    RR_, KK_, VV_ = w(4096, 8, T), w(6144, 8, T), w(8192, 8, T)
    Z = w(10240, 16, T)
    G = w(14336, 32, T)
    M1 = w(0, DC, T)
    O1 = w(4096, DC, T)
    QA, KVA = w(14336, 4, T), w(15360, 4, T)
    QAN, KVAN = w(16384, 4, T), w(17408, 4, T)
    QN, QR, KN = w(18432, 8, T), w(20480, 8, T), w(22528, 8, T)
    VM = w(24576, 2, WIDTH)
    KR, KR2, RT = w(26624, T), w(26880, T), w(27136, 4, T)
    QRAW = w(28160, 4, T)
    PB = w(29184, 2, 2, T)
    PT = w(30208, 2, 2, T)
    SM = w(31232, 64)
    SQ = w(31296, DC, T)
    PADS = w(35392, 2, 4, T + 2)
    SH = w(37456, 2, 4, T)
    NKK = X[:, 0:8, :]
    TW = X[:, 8:12, :]
    SG1 = X[:, 12:16, :]
    LW = X[:, 14:16, :].rearrange("p a (b n) -> p (a b) n", b=2)

    at = 22528
    BK = w(at, 8, 4, CH); at += 2048
    AR = w(at, 8, 3, CH); at += 1536
    BKT = w(at, 2, 2, 4, P); at += 2048
    AK = w(at, 8, P); at += 1024
    RRM = w(at, 2, 2, 4, CH); at += 1024
    SV = w(at, 8, 2, P); at += 2048
    VV = w(at, 4, CH); at += 256
    US = w(at, 2, CH); at += 128
    ST = w(at, 2, CH); at += 128
    SBD = w(at, 2, P); at += 256
    STMP = w(at, 2, CH); at += 128
    EP = w(at, 2, T); at += 512
    RC, KC, NC_ = w(at, T), w(at + 256, T), w(at + 512, T); at += 768
    VD = w(at, 4, 2, CH); at += 512
    RB = w(at, T); at += 256
    PP = w(at, 8); at += 8
    XY = w(at, 2, 2, 4, P)
    LS = w(at + 2048, 2, 4, P)
    ZS = w(at + 3072, 2, 4, P)
    SG = w(at, 4, T)
    CSUM, EN, EM = w(at + 1024, 2, T), w(at + 1536, 2, T), w(at + 2048, 2, T)
    KD, BD, TM = w(at + 2560, 2, T), w(at + 3072, 2, T), w(at + 3584, 2, T)
    at += 4096
    assert at <= WORK, at

    UPAD = w(0, 8, T + TAPS - 1)
    ACC = w(2304, 8, T)
    MIX = w(4352, DC, T)
    SQ2 = w(8448, DC, T)
    PTM, FTM = w(12544, 2, COLS), w(13568, 2, COLS)
    PL, FC, ZF = w(14592, 4, T), w(15616, 4, 2, T), w(17664, 4, T)
    SGB, TB, TB2 = w(18688, 4, T), w(19712, 4, T), w(12544, 4, T)
    PRE = w(12544, DC, T)
    HID_HI, HID_LO = own("hid_hi", 0, 44, T), own("hid_lo", 11264, 44, T)
    X_HI, X_LO = own("x_hi", 22528, DC, T), own("x_lo", 26624, DC, T)
    GU, GU2, GU3 = w(30720, 4, T), w(31744, 4, T), own("gu", 32768, 4, T, dt=F32)
    P2, P2_HI, P2_LO = w(33792, 2, T), own("p_hi", 34304, 2, T), own("p_lo", 33792, 2, T)
    BROW = w(36608, 2 * COLS)
    HI = own("ring_hi", 35504, 4, SLOT // 2)

    Q_SB, K_SB, V_SB = w(4096, 8, T), w(6144, 8, T), w(8192, 2, WIDTH)
    Q_DS, K_DS, K_IX = w(10240, 8, T), w(12288, T), w(12544, 2, T)
    V_DS, W_IX, Q_IX = w(13056, 2, P), w(13312, 2, IDX_HEADS), w(13376, 8, T)
    SBB = w(15424, 2, 4, 4, TRI)
    ROT = w(27712, 4, T)
    ANG = w(28736, 4, T)
    TURN, TURNI = w(29760, 4, T), w(29760, 4, T).bitcast(I32)
    O3 = w(30784, DC, T)
    REL, LG, PTR = w(34880, 4, TRI), w(34880, 4, TRI), w(36416, 4, TRI)
    SCORE, LEFT, SBIAS = w(37952, TRI), w(38336, TRI), w(38720, TRI)
    TOP, SM3 = w(39104, 8), w(39112, 64)
    SQ3 = w(15424, DC, T)
    NORM3 = w(19520, DC, T)
    HID3_HI, HID3_LO = own("hid3_hi", 4096, FF3_CHUNKS, T), own("hid3_lo", 15360, FF3_CHUNKS, T)
    H3_HI, H3_LO = own("h3_hi", 26624, DC, T), own("h3_lo", 0, DC, T)
    UP3 = w(30720, 8, T + 2)
    UC = own("uc", 32784, 8, T, dt=F32)
    GSIG = UP3[:, 0:4, 2:T + 2]
    OUT = w(25680, DC, T)

    ADA = [(w(18432, ADA_RING, SLOT), w(22528, ADA_SUMS, COLS), w(24576, 2, COLS)),
           (w(24832, ADA_RING, SLOT), w(28928, ADA_SUMS, COLS), w(35392, 2, COLS))]

    block = ctx.enter_context(nc.Block())

    @block.sync
    def _(sp):
        sp.dma_start(X[:, :, :], a["x"]).then_inc(S("x_loaded"), 16)
        for k in range(RING):
            sp.dma_start(ring[:, k, :], a["weights"][k]).then_inc(loaded[k], 16)
        def trips(first, count, ada=None):
            with sp.Fori(0, count) as i:
                for k in range(RING):
                    sp.wait_ge(w_used, i * RING + first - RING + k + 1)
                    sp.dma_start(ring[:, k, :],
                                 a["weights"][bass.ds(i * RING + first + k, 1), :, :].rearrange("a p n -> (a p) n"))\
                        .then_inc(loaded[k], 16)
                    if ada:
                        n, buffers = 4 * ada[0] + k, ada[1]
                        sp.wait_ge(S("ada_used"), i * 4 + n + 1)
                        sp.dma_start(buffers[:, k % ADA_RING, :],
                                     a["ada"][bass.ds(i * 4 + n, 1), :, :].rearrange("a p n -> (a p) n"))\
                            .then_inc(S(f"ada_loaded{k % ADA_RING}"), 16)

        at_, done = RING, 0
        for k, (first, groups) in enumerate(ADA_RUNS):
            if first > at_:
                trips(at_, (first - at_) // RING)
            trips(first, groups, (done, ADA[k][0]))
            at_, done = first + 4 * groups, done + groups
        trips(at_, (SLOTS - at_) // RING)
        for n in range(SLOTS - (SLOTS - at_) % RING, SLOTS):
            sp.wait_ge(w_used, n - RING + 1)
            sp.dma_start(ring[:, n % RING, :], a["weights"][n]).then_inc(loaded[n % RING], 16)
        for k in range(4):
            sp.wait_ge(S("out_ready"), k + 1)
            sp.dma_start(a["out"][:, 4 * k:4 * k + 4, :], OUT[:, 4 * k:4 * k + 4, :]).then_inc(S("out_stored"), 16)
        sp.wait_ge(S("out_stored"), 64)

    @block.tensor
    def _(pe):
        t = Tally(pe)
        mm = pe.matmul

        def weights(n, i=None, step=0):
            v = 16 * (n // RING + 1)
            pe.wait_ge(loaded[n % RING], v if i is None else v + i * (16 * step // RING))
            return ring[:, n % RING, :]

        def banks_free(name, j, i=None, step=0):
            p, n = PAIR[name, j]
            if n > 1:
                pe.wait_ge(read_out[p], n - 1 if i is None else n - 1 + i * step)
            return 2 * p

        def by_feature(n, per, rhs, b, i=None, step=0, k0=0, last=None, tiles=4):
            last = k0 + per * KPS if last is None else last
            for s in range(per):
                ws = weights(n + s, i, step).rearrange("p (k c) -> p k c", k=KPS)
                ks = [k for k in range(KPS) if k0 + s * KPS + k < last]
                for k in ks:
                    kc = k0 + s * KPS + k
                    for m in range(tiles):
                        ins = mm(PS[:, b + m // 2, (m % 2) * T:(m % 2 + 1) * T], ws[:, k, m * P:(m + 1) * P], rhs(kc),
                                 start=(kc == 0 and m % 2 == 0), stop=(kc == last - 1), skip_group_check=True)
                ins.then_inc(w_used, 1)

        def by_parts(n, per, hi, lo, b, i=None, step=0, k0=0, last=None, ks=range(KPS)):
            last = k0 + per * len(ks) if last is None else last
            for s in range(per):
                e = SPLIT_AT[n + s]
                w_lo = ring_parts[:, (n + s) % RING, :].rearrange("p (k c) -> p k c", k=KPS)
                for half in range(2):
                    v = 2 * e + half + 1
                    pe.wait_ge(S("lo_ready"), v if i is None else v + i * 2 * step)
                    w_hi = HI[:, 2 * (e % 2) + half, :].rearrange("p (k c) -> p k c", k=KPS // 2)
                    for k in range(KPS // 2):
                        if 2 * half + k not in ks:
                            continue
                        kc = k0 + s * len(ks) + ks.index(2 * half + k)
                        if kc >= last:
                            continue
                        for m in range(4):
                            o = PS[:, b + m // 2, (m % 2) * T:(m % 2 + 1) * T]
                            cols = slice(m * P, (m + 1) * P)
                            mm(o, w_hi[:, k, cols], hi(kc), start=(kc == 0 and m % 2 == 0), stop=False, skip_group_check=True)
                            mm(o, w_hi[:, k, cols], lo(kc), start=False, stop=False, skip_group_check=True)
                            ins = mm(o, w_lo[:, 2 * half + k, cols], hi(kc), start=False, stop=(kc == last - 1),
                                     skip_group_check=True)
                    ins.then_inc(S("half_used") if half == 0 else w_used, 1)

        def by_token(n, per, lhs, b, i=None, step=0, biased=False):
            for s in range(per):
                ws = weights(n + s, i, step).rearrange("p (k c) -> p k c", k=KPS)
                for k in range(KPS):
                    kc = s * KPS + k
                    for m in range(2):
                        ins = mm(PS[:, b + m, :], lhs(kc, m), ws[:, k, :], start=(kc == 0 and not biased),
                                 stop=(kc == per * KPS - 1), skip_group_check=True)
                ins.then_inc(w_used, 1)

        def sum_over_features(bank, k):
            t.wait(S("red_ready"), 1)
            t.give(mm(PS[:, bank, 0:T], ones, RED[:, k, :], start=True, stop=True), S("sum_ready"))

        def ada_sum(g):
            run = 0 if g < ADA_RUNS[0][1] else 1
            t.wait(S("ada_partial"), 1)
            col = 4 * (g % 8) if run == 0 else 4 * ((g - 8) % 12)
            for m in range(4):
                ins = mm(PS[:, 7, col + m:col + m + 1], ADA[run][1][:, g % ADA_SUMS, m * P:(m + 1) * P], ones[:, 0:1],
                         start=True, stop=True, skip_group_check=True)
            t.give(ins, S("ada_summed"))

        t.give(pe.nop(), S("ada_summed"), ADA_SUMS)
        h = lambda k: H[:, k, :]
        pe.wait_ge(S("const_loaded"), 32)
        sum_over_features(4, 0)
        t.wait(S("h_ready"), DC)
        by_feature(slot0("qa"), 4, h, banks_free("qa", 0))
        by_feature(slot0("kva"), 4, h, banks_free("kva", 0))
        b = banks_free("kr", 0)
        ws = weights(slot0("kr")).rearrange("p (k c) -> p k c", k=DC)
        for k in range(DC):
            ins = mm(PS[:, b, 0:T], ws[:, k, :], H[:, k, :], start=(k == 0), stop=(k == DC - 1))
        ins.then_inc(w_used, 1)
        by_feature(slot0("lora"), 4, h, banks_free("lora", 0))
        sum_over_features(4, 1)
        sum_over_features(5, 0)
        t.wait(S("kr_copied"), 1)
        t.give(mm(PS[:, 6, 0:T], con("swap", P), KR, start=True, stop=True), S("swapped"))
        ada_sum(0)
        for j in range(6):
            by_feature(slot0("rkv", j), 4, h, banks_free("rkv", j))
            ada_sum(1 + j)
        by_feature(slot0("z", 0), 4, h, banks_free("z", 0))
        ada_sum(7)
        by_feature(slot0("z", 1), 4, h, banks_free("z", 1))
        t.wait(S("kk_squared"), 1)
        t.wait(S("kr_rotated"), 1)
        t.wait(S("ada_read"), 1)
        for n in range(4):
            ins = mm(PS[:, 4 + n, :], con("bones", P), w(31296, 4, 512)[:, n, :], start=True, stop=True)
        t.give(ins, S("kk_summed"))
        t.wait(S("latents_ready"), 2)
        qan, kvan = (lambda k: QAN[:, k, :]), (lambda k: KVAN[:, k, :])
        for j in range(2):
            by_feature(slot0("q_nope", j), 1, qan, banks_free("q_nope", j))
        by_feature(slot0("q_rope"), 1, qan, banks_free("q_rope", 0))
        for j in range(2):
            by_feature(slot0("k_nope", j), 1, kvan, banks_free("k_nope", j))
        for j in range(2):
            by_token(slot0("v_mla", j), 1, lambda k, m: KVAN[:, k, m * P:(m + 1) * P], banks_free("v_mla", j))
        t.wait(S("kk_rooted"), 1)
        t.wait(S("qraw_copied"), 1)
        for m in range(2):
            ins = mm(PS[:, 6 + m, :], con("swap", P), QRAW[:, 2 * m:2 * m + 2, :], start=True, stop=True)
        t.give(ins, S("swapped"))
        t.wait(S("mla_ready"), 1)
        for hd in range(HEADS + 1):
            if hd < HEADS:
                b = 4 + hd % 2
                if hd >= 2:
                    t.wait(S("exp_done"), 2)
                for q in range(2):
                    o = PS[:, b, q * T:(q + 1) * T]
                    mm(o, QN[:, hd, q * P:(q + 1) * P], KN[:, hd, :], start=(q == 0), stop=False, skip_group_check=True)
                    ins = mm(o, QR[:, hd, q * P:(q + 1) * P], KR2, start=False, stop=True, skip_group_check=True)
                t.give(ins, S("scores_ready"))
            if hd >= 1:
                g = hd - 1
                t.wait(S("probs_ready"), 1)
                if g >= 1:
                    t.wait(S("pt_copied"), 1)
                for kt in range(2):
                    for q in range(2):
                        ins = pe.transpose(PS[:, 6, kt * T + q * P:kt * T + (q + 1) * P],
                                           PB[:, g % 2, q, kt * P:(kt + 1) * P], ident)
                t.give(ins, S("pt_ready"))
                if g in (2, 5):
                    j = (g - 2) // 3
                    by_feature(slot0("z2", j), 4, h, banks_free("z2", j))
                pe.wait_ge(S("pt_copied"), g + 1)
                if g >= 1:
                    t.wait(S("y_mla_ready"), 1)
                for kt in range(2):
                    ins = mm(PS[:, 7, 0:T], VM[:, kt, g * P:(g + 1) * P], PT[:, g % 2, kt, :],
                             start=(kt == 0), stop=(kt == 1))
                t.give(ins, S("pv_ready"))
        t.wait(S("pt_copied"), 1)
        t.wait(S("zeros_ready"), 1)
        sm = {S(k): v for k, v in dict(lw_loaded=16, staged=1, pair_done=1, lora_mm=1, vt_ready=1, l_mm=2, gram_mm=2, bkt_mm=2,
                                       tilde_ready=1, l_read=2, y_init=2, gram_read=4, bkt_read=4, x_init=2, vt_read=1,
                                       z_ready=10, z_mm=10, xy_mm=12, xy_ready=10, u_ready=8, u_mm=8,
                                       sa_ready=8, sa_mm=8, s_ready=6, s_mm=6, y_mm=1).items()}
        with pe.Fori(0, PAIRS) as i:
            t.enter(i, sm)
            t.wait(S("lw_loaded"), 16)
            t.wait(S("pair_done"), 1)
            for k in range(4):
                ins = mm(PS[:, 4 + k // 2, (k % 2) * T:(k % 2 + 1) * T], LW[:, k, :], TW[:, k, :], start=True, stop=True)
            t.give(ins, S("lora_mm"))
            t.wait(S("staged"), 1)
            for c in range(4):
                ins = pe.transpose(PS[:, 6, c * P:(c + 1) * P], VD[:, c, :, :].rearrange("p a b -> p (a b)"), ident)
            t.give(ins, S("vt_ready"))
            by_feature(slot0("gates"), 4, h, banks_free("gates", 0, i, 1), i, 4)
            t.wait(S("tilde_ready"), 1)
            t.wait(S("vt_read"), 1)
            for d in range(2):
                if d == 1:
                    t.wait(S("l_read"), 1)
                for c in range(4):
                    e = 4 * d + c
                    ins = mm(PS[:, 4, c * P:(c + 1) * P], AR[:, e, 0:2, :].rearrange("p a b -> p (a b)"),
                             BK[:, e, 0:4:3, :], start=True, stop=True)
                t.give(ins, S("l_mm"))
                if d == 1:
                    t.wait(S("gram_read"), 2)
                for c in range(4):
                    e = 4 * d + c
                    mm(PS[:, 2, c * P:(c + 1) * P], BK[:, e, 0:2, :].rearrange("p a b -> p (a b)"),
                       AR[:, e, 0:3:2, :], start=True, stop=True)
                    ins = mm(PS[:, 3, c * P:(c + 1) * P], BK[:, e, 2:4, :].rearrange("p a b -> p (a b)"),
                             AR[:, e, 1:3, :], start=True, stop=True)
                t.give(ins, S("gram_mm"))
                if d == 1:
                    t.wait(S("bkt_read"), 2)
                for c in range(4):
                    e = 4 * d + c
                    for hh in range(2):
                        ins = pe.transpose(PS[:, 6 + hh, c * P:(c + 1) * P],
                                           BK[:, e, 2 * hh:2 * hh + 2, :].rearrange("p a b -> p (a b)"), ident)
                t.give(ins, S("bkt_mm"))
                t.wait(S("y_init"), 1)
                if d == 1:
                    t.wait(S("x_init"), 1)
                for c in range(4):
                    ins = pe.transpose(PS[:, 5, c * P:(c + 1) * P], XY[:, d, 1, c, :], ident)
                t.give(ins, S("xy_mm"))
            t.wait(S("x_init"), 1)
            t.wait(S("l_read"), 1)
            t.wait(S("gram_read"), 2)
            t.wait(S("bkt_read"), 2)
            for l in range(2, 7):
                for d in range(2):
                    if l > 2:
                        t.wait(S("xy_ready"), 1)
                    for c in range(4):
                        ins = mm(PS[:, 2 + 3 * d, c * P:(c + 1) * P], LS[:, d, c, :], XY[:, d, 0, c, :], start=True, stop=True)
                    t.give(ins, S("z_mm"))
                for d in range(2):
                    t.wait(S("z_ready"), 1)
                    for c in range(4):
                        ins = mm(PS[:, 3 + 3 * d, c * P:(c + 1) * P], XY[:, d, 1, c, :], ZS[:, d, c, :], start=True, stop=True)
                    if l < 6:
                        for c in range(4):
                            ins = mm(PS[:, 4 + 3 * d, c * P:(c + 1) * P], ZS[:, d, c, :], XY[:, d, 1, c, :], start=True, stop=True)
                    t.give(ins, S("xy_mm"))
            for k in range(4):
                for d in range(2):
                    c = k if d == 0 else 3 - k
                    e = 4 * d + c
                    if k == 0:
                        t.wait(S("xy_ready"), 1)
                    else:
                        t.wait(S("s_ready"), 1)
                    o = PS[:, 3 + d, 0:CH]
                    ins = mm(o, AK[:, e, :], VV[:, c, :], start=True, stop=(k == 0))
                    if k > 0:
                        ins = mm(o, AR[:, e, 0:2, :].rearrange("p a b -> p (a b)"), ST[:, d, :], start=False, stop=True)
                    t.give(ins, S("u_mm"))
                for d in range(2):
                    c = k if d == 0 else 3 - k
                    t.wait(S("u_ready"), 1)
                    t.give(mm(PS[:, 3 + d, CH:2 * CH], XY[:, d, 0, c, :], US[:, d, :], start=True, stop=True), S("sa_mm"))
                for d in range(2):
                    c = k if d == 0 else 3 - k
                    e = 4 * d + c
                    t.wait(S("sa_ready"), 1)
                    y = PS[:, 2, c * CH:(c + 1) * CH]
                    if k > 0:
                        mm(y, SBD[:, d, :], AR[:, e, 2, :], start=False, stop=False, skip_group_check=True)
                    for hh in range(2):
                        ins = mm(y, SV[:, e, hh, :], RRM[:, d, hh, c, :], start=(k == 0 and d == 0 and hh == 0),
                                 stop=True, skip_group_check=True)
                    if k == 3 and d == 1:
                        t.give(ins, S("y_mm"))
                    if k < 3:
                        for hh in range(2):
                            ins = mm(PS[:, 3 + d, 2 * CH:3 * CH], BKT[:, d, hh, c, :], SV[:, e, hh, hh * CH:(hh + 1) * CH],
                                     start=(hh == 0), stop=(hh == 1))
                        t.give(ins, S("s_mm"))
            t.leave(PAIRS)
        yf = RR_.rearrange("p c t -> p (c t)")
        t.wait(S("pair_done"), 1)
        t.wait(S("y_stored"), PAIRS)
        for n in range(4):
            ins = mm(PS[:, 4 + n, :], con("bones", P), yf[:, n * 512:(n + 1) * 512], start=True, stop=True)
        t.give(ins, S("gn_mm"))
        zm = lambda k: Z[:, k, :]
        by_feature(slot0("br_mla", 0), 2, zm, banks_free("br_mla", 0))
        t.wait(S("gn_squared"), 1)
        sqf = w(31296, 4, 512)
        for n in range(4):
            ins = mm(PS[:, 4 + n, :], con("bones", P), sqf[:, n, :], start=True, stop=True)
        t.give(ins, S("gn_mm"))
        by_feature(slot0("br_mla", 1), 2, zm, banks_free("br_mla", 1))
        t.wait(S("gn_rooted"), 1)
        kf = KK_.rearrange("p c t -> p (c t)")
        for n in range(4):
            ins = mm(PS[:, 4 + n, :], con("bones", P), kf[:, n * 512:(n + 1) * 512], start=True, stop=True)
        t.give(ins, S("gn_mm"))
        for j in range(2, 4):
            by_feature(slot0("br_mla", j), 2, zm, banks_free("br_mla", j))
        t.wait(S("y_rwkv_ready"), 1)
        for j in range(4):
            by_feature(slot0("br_rwkv", j), 2, lambda k: Z[:, 8 + k, :], banks_free("br_rwkv", j))
            if j % 2 == 1:
                ada_sum(8 + j // 2)
        t.wait(S("merged_ready"), 1)
        for j in range(4):
            by_feature(slot0("w_out", j), 4, lambda k: M1[:, k, :], banks_free("w_out", j))
            ada_sum(10 + j)
        sum_over_features(4, 0)
        xc = lambda k: X[:, k, :]
        pe.wait_ge(S("x_ready"), 1)
        for j in range(4):
            by_feature(slot0("conv_in", j), 4, xc, banks_free("conv_in", j))
            ada_sum(14 + j)
        pe.wait_ge(S("par2_loaded"), 64)
        for k, nm in enumerate(("pool_in", "four_in")):
            b = banks_free(nm, 0)
            for m in range(2):
                mm(PS[:, b + m, :], ones[0:1, :], BROW[0:1, k * COLS:(k + 1) * COLS], start=True, stop=False,
                   skip_group_check=True)
            by_token(slot0(nm), 4, lambda k, m: X[:, k, m * P:(m + 1) * P], b, biased=True)
            ada_sum(18 + k)
        ws = weights(slot0("poolmat")).rearrange("p (k g n) -> p k g n", k=2, g=4)
        pe.wait_ge(S("ptm_copied"), 1)
        pe.wait_ge(S("rooted"), t.value(S("sum_ready")))
        for g in range(4):
            for kt in range(2):
                ins = mm(PS[:, 4 + g // 2, (g % 2) * T:(g % 2 + 1) * T], PTM[:, kt, g * P:(g + 1) * P], ws[:, kt, g, :],
                         start=(kt == 0), stop=(kt == 1))
        ins.then_inc(w_used, 1)
        ws = weights(slot0("seqmat"))
        dft = ws[:, 512:1536].rearrange("p (k n) -> p k n", k=2)
        pe.wait_ge(S("ptm_copied"), 2)
        t.wait(S("ada_read"), 1)
        for hd in range(4):
            if hd == 2:
                pe.wait_ge(S("pl_copied"), 1)
            b = (6, 7, 4, 5)[hd]
            for kt in range(2):
                ins = mm(PS[:, b, :], FTM[:, kt, hd * P:(hd + 1) * P], dft[:, kt, :], start=(kt == 0), stop=(kt == 1))
            ins.then_inc(S("dft_mm"), 1)
        pe.wait_ge(S("fc_copied"), 2)
        for g in range(4):
            ins = mm(PS[:, 6 + g // 2, (g % 2) * T:(g % 2 + 1) * T], ws[:, g * P:(g + 1) * P], PL[:, g, :], start=True, stop=True)
        ins.then_inc(S("pool_mm"), 1)
        pe.wait_ge(S("fc_copied"), 4)
        for hp in range(2):
            mm(PS[:, 4 + hp, :], ws[:, 1536:1536 + P], FC[:, 2 * hp:2 * hp + 2, 0, :], start=True, stop=False)
            ins = mm(PS[:, 4 + hp, :], ws[:, 1536 + P:1536 + 2 * P], FC[:, 2 * hp:2 * hp + 2, 1, :], start=False, stop=True)
        ins.then_inc(w_used, 1)
        ws = weights(slot0("four_w"))
        pe.wait_ge(S("zf_copied"), 1)
        pe.wait_ge(S("pool_done"), 1)
        for hd in range(4):
            ins = mm(PS[:, 6 + hd // 2, (hd % 2) * T:(hd % 2 + 1) * T], ws[:, hd * P:(hd + 1) * P], ZF[:, hd, :],
                     start=True, stop=True)
        ins.then_inc(w_used, 1)
        sum_over_features(4, 0)
        sum_over_features(5, 1)
        t.wait(S("mix_ready"), 1)
        for j in range(4):
            by_feature(slot0("w_out2", j), 4, lambda k: MIX[:, k, :], banks_free("w_out2", j))
            ada_sum(20 + j)
        sum_over_features(4, 0)
        sum_over_features(5, 1)
        pe.wait_ge(S("split_done"), 1)
        x_hi, x_lo = (lambda k: X_HI[:, k, :]), (lambda k: X_LO[:, k, :])
        with pe.Fori(0, 11) as i:
            for j in range(2):
                by_parts(slot0("ffn2", j), 4, x_hi, x_lo, banks_free("ffn2", j, i, 1), i, 8)
        pe.wait_ge(S("hid_ready"), 12)
        with pe.Fori(0, 4) as i:
            n = slot0("down2")
            by_parts(n, 11, lambda k: HID_HI[:, k, :], lambda k: HID_LO[:, k, :], banks_free("down2", 0, i, 1), i, 16)
            by_parts(n + 11, 4, x_hi, x_lo, banks_free("ple_gate", 0, i, 1), i, 16)
            pe.wait_ge(S("ple_read"), i + 1)
            by_parts(n + 15, 1, lambda k: P2_HI[:, k, :], lambda k: P2_LO[:, k, :], 4, i, 16, ks=(0, 2))
        sum_over_features(4, 0)
        sum_over_features(5, 1)
        sum_over_features(4, 0)
        pe.wait_ge(S("h3_ready"), DC)
        b = banks_free("misc", 0)
        for s in range(4):
            ws = weights(slot0("misc") + s).rearrange("p (k c) -> p k c", k=KPS)
            for k in range(KPS):
                kc = s * KPS + k
                two = ws[:, k, :].rearrange("p (a b c) -> p a b c", a=2, b=2)
                for m in range(2):
                    mm(PS[:, b, m * T:(m + 1) * T], two[:, m, 0, :], H[:, kc, :], start=(kc == 0 and m == 0),
                       stop=(kc == DC - 1), skip_group_check=True)
                for m in range(2):
                    ins = mm(PS[:, b + 1, m * T:(m + 1) * T], H[:, kc, m * P:(m + 1) * P], two[:, :, 1, :],
                             start=(kc == 0 and m == 0), stop=(kc == DC - 1), skip_group_check=True)
            ins.then_inc(w_used, 1)

        def turn(src, swap, n, bank):
            for m in range(0, n, 2):
                k = min(2, n - m)
                ins = mm(PS[:, bank + m // 2, 0:k * T].rearrange("p (c t) -> p c t", t=T), con(swap, P), src[:, m:m + k, :],
                         start=True, stop=True)
            return ins

        def indexer(q):
            if q > 0:
                pe.wait_ge(S("rel_read"), q)
            for n in range(4):
                hd = 4 * q + n
                for m in range(2):
                    ins = mm(PS[:, 4 + n, m * P:m * T + P], Q_IX[:, hd // 2, m * P:(m + 1) * P],
                             K_IX[:, hd % 2, 0:(m + 1) * P], start=(m == 0), stop=True, skip_group_check=True)
            t.give(ins, S("rel_mm"))

        def sb_scores(q):
            for n in range(4):
                hd = 4 * q + n
                for m in range(2):
                    ins = mm(PS[:, 4 + n, m * T:T + m * P], K_SB[:, hd, m * P:(m + 1) * P], Q_SB[:, hd, m * P:T],
                             start=(m == 0), stop=True, skip_group_check=True)
            t.give(ins, S("sb_mm"))

        def sb_suffix(q):
            pe.wait_ge(S("sb_softplus"), q + 1)
            for n in range(4):
                mm(PS[:, 4 + n, 0:T], con("tri", P), SBB[:, q, 2, n, 0:T], start=True, stop=False, skip_group_check=True)
                mm(PS[:, 4 + n, P:T], ones, SBB[:, q, 2, n, T:TRI], start=False, stop=True, skip_group_check=True)
                ins = mm(PS[:, 4 + n, T:TRI], con("tri", P), SBB[:, q, 2, n, T:TRI], start=False, stop=True,
                         skip_group_check=True)
            t.give(ins, S("sb_mm"))

        def sb_out(q):
            pe.wait_ge(S("sb_weights"), q + 1)
            for n in range(4):
                hd = 4 * q + n
                o = PS[:, 4 + n // 2, (n % 2) * T:(n % 2 + 1) * T]
                mm(o, V_SB[:, 0, hd * P:(hd + 1) * P], SBB[:, q, 3, n, 0:T], start=(n % 2 == 0), stop=False,
                   skip_group_check=True)
                ins = mm(o[:, P:T], V_SB[:, 1, hd * P:(hd + 1) * P], SBB[:, q, 3, n, T:TRI], start=False, stop=True,
                         skip_group_check=True)
            t.give(ins, S("sb_mm"))

        by_feature(slot0("q_ix", 0), 4, h, banks_free("q_ix", 0))
        pe.wait_ge(S("misc_copied"), 1)
        pe.wait_ge(S("rooted"), t.value(S("sum_ready")))
        turn(K_DS.unsqueeze(1), "swap128", 1, 4)
        turn(K_IX[:, 0:1, :], "swap64", 1, 5).then_inc(S("turned"), 1)
        by_feature(slot0("q_ix", 1), 4, h, banks_free("q_ix", 1))
        for j in range(2):
            p, n = PAIR["q_ix", j]
            pe.wait_ge(read_out[p], n)
            turn(Q_IX[:, 4 * j:4 * j + 4, :], "swap64", 4, 6).then_inc(S("turned"), 1)
            by_feature(slot0("qk_sb", j), 4, h, banks_free("qk_sb", j))
            pe.wait_ge(S("turn_read"), j + 2)
        pe.wait_ge(S("turn_done"), 3)
        indexer(0)
        by_feature(slot0("qk_sb", 2), 4, h, banks_free("qk_sb", 2))
        indexer(1)
        indexer(2)
        indexer(3)
        by_feature(slot0("qk_sb", 3), 4, h, banks_free("qk_sb", 3))
        pe.wait_ge(S("rel_read"), 4)
        for j in range(2):
            p, n = PAIR["qk_sb", 2]
            pe.wait_ge(read_out[p], n)
            if j == 1:
                pe.wait_ge(S("sb_stored"), 1)
                p, n = PAIR["qk_sb", 3]
                pe.wait_ge(read_out[p], n)
            sb_scores(j)
            by_token(slot0("v_q", 2 * j), 4, lambda k, m: H[:, k, m * P:(m + 1) * P], banks_free("v_q", 2 * j))
            sb_suffix(j)
            by_feature(slot0("v_q", 2 * j + 1), 4, h, banks_free("v_q", 2 * j + 1))
            p, n = PAIR["v_q", 2 * j]
            pe.wait_ge(read_out[p], n)
            sb_out(j)
        for j in range(2):
            p, n = PAIR["v_q", 2 * j + 1]
            pe.wait_ge(read_out[p], n)
            if j == 1:
                pe.wait_ge(S("turn_read"), 4)
            turn(Q_DS[:, 4 * j:4 * j + 4, :], "swap128", 4, 6).then_inc(S("turned"), 1)
        pe.wait_ge(S("sb_stored"), 2)
        pe.wait_ge(S("turn_read"), 5)
        for q in range(2):
            pe.wait_ge(S("turn_done"), 4 + q)
            if q == 1:
                pe.wait_ge(S("ds_stored"), 1)
            for n in range(4):
                for m in range(2):
                    ins = mm(PS[:, 4 + n, m * P:m * T + P], Q_DS[:, 4 * q + n, m * P:(m + 1) * P], K_DS[:, 0:(m + 1) * P],
                             start=(m == 0), stop=True, skip_group_check=True)
            t.give(ins, S("ds_mm"))
            pe.wait_ge(S("ds_probs"), q + 1)
            for n in range(4):
                for src, dst in ((0, 0), (P, P), (2 * P, T)):
                    ins = pe.transpose(PS[:, 4 + n, dst:dst + P], LG[:, n, src:src + P], ident)
            t.give(ins, S("ds_mm"))
            pe.wait_ge(S("ds_turned"), q + 1)
            for n in range(2):
                o = PS[:, 4 + n, :].rearrange("p (c t) -> p c t", t=T)
                mm(o, V_DS[:, 0, :], PTR[:, 2 * n:2 * n + 2, 0:T], start=True, stop=False, skip_group_check=True)
                ins = mm(o[:, :, P:T], V_DS[:, 1, :], PTR[:, 2 * n:2 * n + 2, T:TRI], start=False, stop=True,
                         skip_group_check=True)
            t.give(ins, S("ds_mm"))
        pe.wait_ge(S("ds_stored"), 2)
        sum_over_features(4, 0)
        sum_over_features(5, 1)
        pe.wait_ge(S("o3_ready"), 2)
        for j in range(4):
            by_feature(slot0("w_out3", j), 4, lambda k: O3[:, k, :], banks_free("w_out3", j))
        sum_over_features(4, 0)
        pe.wait_ge(S("split_done"), 2)
        with pe.Fori(0, 11) as i:
            for j in range(2):
                by_parts(slot0("ffn3", j), 4, lambda k: H3_HI[:, k, :], lambda k: H3_LO[:, k, :],
                         banks_free("ffn3", j, i, 1), i, 8)
        pe.wait_ge(S("hid_ready"), 23)
        for j in range(4):
            by_parts(slot0("down3", j), 11, lambda k: HID3_HI[:, k, :], lambda k: HID3_LO[:, k, :],
                     banks_free("down3", j), last=FF3 // P)
        sum_over_features(4, 0)

    @block.scalar
    def _(act):
        t = Tally(act)
        A = act.activation

        def root(bank, k, scale, eps):
            t.wait(S("sum_ready"), 1)
            t.give(A(STD[:, k, :], PS[:, bank, 0:T], ACT.Sqrt, bias=con("eps", 1, eps), scale=scale), S("rooted"))

        def group_done(name, j, i=None, step=0):
            n = used(name, j)
            act.wait_ge(w_used, n if i is None else n + i * step)

        def bank2(p):
            return PS[:, 2 * p:2 * p + 2, :].rearrange("p b n -> p (b n)")

        def split(first, count, i=None, step=0):
            for n in range(first, first + count):
                e = SPLIT_AT[n]
                r = 0 if i is None else i * step
                act.wait_ge(loaded[n % RING], 16 * (n // RING + 1) + (0 if i is None else i * (16 * step // RING)))
                for half in range(2):
                    if e >= 2:
                        if half == 0:
                            act.wait_ge(S("half_used"), e - 1 + r)
                        else:
                            act.wait_ge(w_used, SPLIT_SLOTS[e - 2] + 1 + r)
                    A(HI[:, 2 * (e % 2) + half, :], ring[:, n % RING, half * (SLOT // 2):(half + 1) * (SLOT // 2)], ACT.Copy)\
                        .then_inc(S("hi_ready"), 1)

        def ada_read(first, count):
            act.wait_ge(S("ada_summed"), ADA_SUMS + first + count)
            A(MOD[:, 4 * first:4 * (first + count)], PS[:, 7, 0:4 * count], ACT.Copy).then_inc(S("ada_read"), 1)

        act.dma_start(CON[:, 0:N_1], a["const1"]).then_inc(S("const_loaded"), 16)
        act.dma_start(PR[:, 0:NPAR[0]], a["params1"]).then_inc(S("const_loaded"), 16)
        act.wait_ge(S("x_loaded"), 16)
        t.give(A(SQ, X[:, :, :], ACT.Square), S("squared"))
        act.wait_ge(S("const_loaded"), 32)
        A(CS[:, :], par("c", 0, DC), ACT.Sigmoid).then_inc(S("c_sig"), 1)
        act.wait_ge(S("const_loaded"), 32)
        root(4, 0, 1.0 / D, 0)
        for nm, dst in (("qa", QA), ("kva", KVA)):
            group_done(nm, 0)
            p, _n = PAIR[nm, 0]
            A(dst.rearrange("p c t -> p (c t)"), bank2(p), ACT.Copy).then_inc(read_out[p], 1)
        act.wait_ge(read_out[0], PAIR["qa", 0][1])
        act.wait_ge(S("h_ready"), 1)
        t.give(A(SQ[:, 0:4, :], QA, ACT.Square), S("squared"))
        act.wait_ge(read_out[1], PAIR["kva", 0][1])
        t.give(A(SQ[:, 4:8, :], KVA, ACT.Square), S("squared"))
        group_done("kr", 0)
        A(KR, PS[:, 2 * PAIR["kr", 0][0], 0:T], ACT.Copy).then_inc(S("kr_copied"), 1)
        A(RT[:, 0, :], PS[:, 2 * PAIR["kr", 0][0], 0:T], ACT.Copy).then_inc(read_out[PAIR["kr", 0][0]], 1)

        def to_pad(name, j, k, i=None, step=0):
            group_done(name, j, i, step)
            p, _n = PAIR[name, j]
            A(PADS[:, k, :, 1:T + 1], PS[:, 2 * p:2 * p + 2, :].rearrange("p b (c t) -> p (b c) t", t=T), ACT.Copy)\
                .then_inc(read_out[p], 1)

        act.wait_ge(S("pads_zeroed"), 1)
        to_pad("lora", 0, 1)
        root(4, 1, 1.0 / RANK, 0)
        root(5, 0, 1.0 / RANK, 0)
        act.wait_ge(S("lora_shifted"), 4)
        A(TW[:, 0:2, :], SG1[:, 0:2, :], ACT.Tanh).then_inc(S("tw_ready"), 1)
        A(TW[:, 2:4, :], SG1[:, 2:4, :], ACT.Copy).then_inc(S("tw_ready"), 1)
        with act.Fori(0, 3) as i:
            for j in range(2):
                act.wait_ge(S("pad_free"), i * 2 + j + 1)
                to_pad("rkv", j, j, i, 8)
        for j in range(2):
            group_done("z", j)
            p, n = PAIR["z", j]
            if j == 1:
                act.wait_ge(S("z_gated"), 1)
            A(SG1.rearrange("p c t -> p (c t)"), bank2(p), ACT.Sigmoid).then_inc(S("z_sig"), 1)
        ada_read(0, 8)
        act.wait_ge(S("kk_scaled"), 1)
        A(w(31296, 8, T), NKK, ACT.Square).then_inc(S("kk_squared"), 1)
        act.wait_ge(S("kk_summed"), 1)
        A(w(33344, 2048), PS[:, 4:8, :].rearrange("p b n -> p (b n)"), ACT.Sqrt).then_inc(S("kk_rooted"), 1)
        act.wait_ge(S("ada_used"), ADA_RING + 4 * ADA_RUNS[0][1])
        act.wait_ge(S("ada_summed"), ADA_SUMS + ADA_RUNS[0][1])
        for nm, dsts in (("q_nope", QN), ("q_rope", QRAW), ("k_nope", KN), ("v_mla", VM)):
            for j in range(1 if nm == "q_rope" else 2):
                group_done(nm, j)
                p, n = PAIR[nm, j]
                if nm == "v_mla":
                    A(VM[:, :, j * 512:(j + 1) * 512], PS[:, 2 * p:2 * p + 2, :], ACT.Copy).then_inc(read_out[p], 1)
                elif nm == "q_rope":
                    A(QRAW, PS[:, 2 * p:2 * p + 2, :].rearrange("p b (c t) -> p (b c) t", t=T), ACT.Copy)\
                        .then_inc(read_out[p], 1)
                    act.wait_ge(read_out[p], n)
                    act.nop().then_inc(S("qraw_copied"), 1)
                else:
                    A(dsts[:, 4 * j:4 * j + 4, :].rearrange("p c t -> p (c t)"), bank2(p), ACT.Copy)\
                        .then_inc(read_out[p], 1)
        act.wait_ge(read_out[1], PAIR["v_mla", 0][1])
        act.wait_ge(read_out[0], PAIR["v_mla", 1][1])
        act.wait_ge(S("q_rotated"), 1)
        act.nop().then_inc(S("mla_ready"), 1)
        for hd in range(HEADS + 1):
            if hd < HEADS:
                act.wait_ge(S("max_ready"), hd + 1)
                if hd >= 2:
                    act.wait_ge(S("pt_ready"), hd - 1)
                for q in range(2):
                    A(PB[:, hd % 2, q, :], PS[:, 4 + hd % 2, q * T:(q + 1) * T], ACT.Exp, bias=SM[:, 4 * (hd % 2) + q:4 * (hd % 2) + q + 1],
                      scale=float(NOPE + ROPE) ** -0.5, accum_out=SM[:, 8 + 4 * (hd % 2) + q:9 + 4 * (hd % 2) + q])\
                        .then_inc(S("exp_done"), 1)
            if hd >= 1:
                g = hd - 1
                act.wait_ge(S("pt_ready"), g + 1)
                if g >= 2:
                    act.wait_ge(S("pv_ready"), g - 1)
                A(PT[:, g % 2, :, :].rearrange("p a b -> p (a b)"), PS[:, 6, :], ACT.Copy).then_inc(S("pt_copied"), 1)
                if g in (2, 5):
                    j = (g - 2) // 3
                    group_done("z2", j)
                    p, n = PAIR["z2", j]
                    act.wait_ge(S("z_gated"), 2 + j)
                    A(SG1.rearrange("p c t -> p (c t)"), bank2(p), ACT.Sigmoid).then_inc(S("z_sig"), 1)
        act.wait_ge(S("z_gated"), 4)
        act.dma_start(LW.rearrange("p a b -> p (a b)"), a["lora2"][0]).then_inc(S("lw_loaded"), 16)
        sm = {S(k): v for k, v in dict(lora_mm=1, prep_sg=4, prep_cs=1, exps_ready=3, staged=1, vt_ready=1, vt_read=1,
                                       bkt_mm=2, bkt_read=4, x_init=2, xy_mm=12, xy_ready=10, y_mm=1, y_stored=1,
                                       lw_loaded=16).items()}
        with act.Fori(0, PAIRS) as i:
            t.enter(i, sm)
            t.wait(S("staged"), 1)
            t.wait(S("lora_mm"), 1)
            for k in range(4):
                t.give(A(SG[:, k, :], PS[:, 4 + k // 2, (k % 2) * T:(k % 2 + 1) * T], ACT.Sigmoid, bias=PP[:, k:k + 1]),
                       S("prep_sg"))
            t.give(act.dma_start(LW.rearrange("p a b -> p (a b)"),
                                 a["lora2"][bass.ds(i + 1, 1), :, :].rearrange("a p n -> (a p) n")), S("lw_loaded"), 16)
            t.wait(S("vt_ready"), 1)
            tv = PS[:, 6, :].rearrange("p (c n) -> p c n", c=4)
            A(VV[0:64, :, :], tv[0:64, :, CH:P], ACT.Copy)
            A(VV[64:128, :, :], tv[64:128, :, 0:CH], ACT.Copy)
            for d in range(2):
                A(SV[64:128, 4 * d:4 * d + 4, 0, 0:CH], tv[64:128, :, 0:CH], ACT.Copy)
                ins = A(SV[0:64, 4 * d:4 * d + 4, 1, CH:P], tv[0:64, :, CH:P], ACT.Copy)
            t.give(ins, S("vt_read"))
            t.wait(S("prep_cs"), 1)
            t.give(A(EP, CSUM, ACT.Exp, scale=-KAPPA), S("exps_ready"))
            t.give(A(EN, CSUM, ACT.Exp, scale=KAPPA), S("exps_ready"))
            t.give(A(EM, EM, ACT.Exp, scale=-KAPPA), S("exps_ready"))
            group_done("gates", 0, i, 4)
            act.wait_ge(S("const_loaded"), 16)
            A(G[:, bass.ds(i * 4, 4), :].rearrange("p c t -> p (c t)"), bank2(0), ACT.Sigmoid).then_inc(read_out[0], 1)
            for d in range(2):
                t.wait(S("bkt_mm"), 1)
                for hh in range(2):
                    t.give(A(BKT[:, d, hh, :, :].rearrange("p a b -> p (a b)"), PS[:, 6 + hh, :], ACT.Copy), S("bkt_read"))
                t.wait(S("xy_mm"), 1)
                t.give(A(XY[:, d, 0, :, :].rearrange("p a b -> p (a b)"), PS[:, 5, :], ACT.Copy), S("x_init"))
            for l in range(2, 7):
                for d in range(2):
                    t.wait(S("xy_mm"), 1)
                    n = 2 if l < 6 else 1
                    t.give(A(XY[:, d, 0:n, :, :].rearrange("p e a b -> p (e a b)"),
                             PS[:, 3 + 3 * d:3 + 3 * d + n, :].rearrange("p b n -> p (b n)"), ACT.Copy), S("xy_ready"))
            t.wait(S("y_mm"), 1)
            act.wait_ge(S("const_loaded"), 16)
            t.give(A(RR_[:, bass.ds(i, 1), :].rearrange("p a t -> p (a t)"), PS[:, 2, 0:T], ACT.Copy), S("y_stored"))
            t.leave(PAIRS)
        act.wait_ge(S("h_ready"), DC)
        act.wait_ge(S("lw_loaded"), 16 * (PAIRS + 1))
        act.wait_ge(S("pair_done"), PAIRS + 1)
        act.wait_ge(S("y_stored"), PAIRS)
        act.dma_start(X[:, :, :], a["x"]).then_inc(S("x_loaded"), 16)
        act.wait_ge(S("gn_centred"), 1)
        A(w(31296, 2048), RR_.rearrange("p c t -> p (c t)"), ACT.Square).then_inc(S("gn_squared"), 1)
        act.wait_ge(S("gn_mm"), 2)
        A(w(33344, 2048), PS[:, 4:8, :].rearrange("p b n -> p (b n)"), ACT.Sqrt, bias=con("eps", 1, 1), scale=1.0 / CH)\
            .then_inc(S("gn_rooted"), 1)
        with act.Fori(0, 2) as i:
            for j in range(2):
                group_done("w_out", j, i, 8)
                p, n = PAIR["w_out", j]
                act.wait_ge(S("const_loaded"), 16)
                A(O1[:, bass.ds(i * 8 + 4 * j, 4), :].rearrange("p c t -> p (c t)"), bank2(p), ACT.Copy).then_inc(read_out[p], 1)
        for j in range(2, 4):
            p, n = PAIR["w_out", j]
            act.wait_ge(read_out[p], n)
        t.give(A(SQ, O1, ACT.Square), S("squared"))
        root(4, 0, 1.0 / D, 0)
        def mean(bank, k, n):
            t.wait(S("sum_ready"), 1)
            t.give(A(STD[:, k, :], PS[:, bank, 0:T], ACT.Copy, scale=1.0 / n), S("rooted"))

        act.wait_ge(S("x_ready"), 1)
        act.dma_start(PR[:, 0:NPAR[1]], a["params2"]).then_inc(S("par2_loaded"), 16)
        act.dma_start(CON[:, N_ALL:N_3], a["const3"]).then_inc(S("par2_loaded"), 16)
        act.dma_start(P2, a["p"]).then_inc(S("par2_loaded"), 16)
        act.dma_start(BROW[0:1, :], a["b_rows"]).then_inc(S("par2_loaded"), 16)
        act.wait_ge(S("par2_loaded"), 64)
        for j in range(2):
            group_done("conv_in", 2 * j)
            if j == 1:
                act.wait_ge(S("conv_u_ready"), 1)
            for m in range(4):
                ins = A(SGB[:, m, :], PS[:, m // 2, (m % 2) * T:(m % 2 + 1) * T], ACT.Sigmoid, bias=par("b_in", 8 + 4 * j + m))
            ins.then_inc(read_out[0], 1)
        for nm, dst in (("pool_in", PTM), ("four_in", FTM)):
            group_done(nm, 0)
            p, n = PAIR[nm, 0]
            A(dst.rearrange("p a b -> p (a b)"), bank2(p), ACT.Copy).then_inc(read_out[p], 1)
            act.wait_ge(read_out[p], n)
            act.nop().then_inc(S("ptm_copied"), 1)
        ada_read(8, 12)
        group_done("poolmat", 0)
        A(PL.rearrange("p a b -> p (a b)"), bank2(2), ACT.Copy).then_inc(S("pl_copied"), 1)
        for hd in range(4):
            act.wait_ge(S("dft_mm"), hd + 1)
            A(FC[:, hd, :, :].rearrange("p a b -> p (a b)"), PS[:, (6, 7, 4, 5)[hd], :], ACT.Copy).then_inc(S("fc_copied"), 1)
        group_done("seqmat", 0)
        A(ZF.rearrange("p a b -> p (a b)"), bank2(2), ACT.Copy).then_inc(S("zf_copied"), 1)
        mean(4, 0, WIDTH)
        t.wait(S("centred"), 1)
        t.give(A(SQ2[:, 0:8, :], ACC, ACT.Square), S("squared"))
        root(5, 1, 1.0 / WIDTH, 2)
        for k in range(8):
            act.wait_ge(S("v_ready"), k + 1)
            A(SQ2[:, 8 + k, :], SQ2[:, k, :], ACT.Sigmoid, bias=par("cln_b", k)).then_inc(S("v_sig"), 1)
        for j in range(4):
            group_done("w_out2", j)
            p, n = PAIR["w_out2", j]
            for m in range(4):
                ins = A(PRE[:, 4 * j + m, :], PS[:, 2 * p + m // 2, (m % 2) * T:(m % 2 + 1) * T], ACT.Identity,
                        bias=par("b_out", 4 * j + m))
            ins.then_inc(read_out[p], 1)
        ada_read(20, 4)
        mean(4, 0, D)
        t.wait(S("centred"), 1)
        t.give(A(SQ2, PRE, ACT.Square), S("squared"))
        root(5, 1, 1.0 / D, 2)
        A(P2_HI, P2, ACT.Copy).then_inc(S("p_hi"), 1)
        split(slot0("ffn2"), 2)
        for k in range(DC):
            act.wait_ge(S("scaled"), k + 1)
            A(X_HI[:, k, :], PRE[:, k, :], ACT.Identity, bias=par("ln1_b", k))
            A(X[:, k, :], PRE[:, k, :], ACT.Identity, bias=par("ln1_b", k)).then_inc(S("x1_ready"), 1)
        with act.Fori(0, 11) as i:
            for j in range(2):
                split(slot0("ffn2", j) + 2, 4, i, 8)
                if j == 0:
                    group_done("ffn2", 0, i, 8)
                    A(GU.rearrange("p c t -> p (c t)"), bank2(0), ACT.Sigmoid).then_inc(S("ffn_sig"), 1)

        def ple_gate(i, ahead):
            split(slot0("down2") + 2, 14, i, 16)
            act.wait_ge(w_used, i * 16 + slot0("down2") + 15)
            A(GU.rearrange("p c t -> p (c t)"), bank2(1), ACT.Sigmoid).then_inc(read_out[1], 1)
            split(slot0("down2") + 16, ahead, i, 16)

        with act.Fori(0, 3) as i:
            ple_gate(i, 2)
        ple_gate(3, 0)
        mean(4, 0, D)
        t.wait(S("centred"), 1)
        t.give(A(SQ2, X[:, :, :], ACT.Square), S("squared"))
        root(5, 1, 1.0 / D, 2)
        for k in range(DC):
            act.wait_ge(S("scaled"), DC + k + 1)
            A(X[:, k, :], X[:, k, :], ACT.Identity, bias=par("ln2_b", k)).then_inc(S("x1_ready"), 1)
        act.wait_ge(S("x1_ready"), 2 * DC)
        act.dma_start(PR[:, 0:NPAR[2]], a["params3"]).then_inc(S("par3_loaded"), 16)
        act.dma_start(TURNI[:, 0, :], a["positions"].broadcast_to([P, T])).then_inc(S("par3_loaded"), 16)
        t.give(A(SQ3, X[:, :, :], ACT.Square), S("squared"))
        root(4, 0, 1.0 / D, 0)

        def modulated(n, shift):
            for k in range(DC):
                act.wait_ge(S("scaled"), (2 + n) * DC + k + 1)
                if n == 1:
                    A(H3_HI[:, k, :], NORM3[:, k, :], ACT.Identity, bias=MOD[:, shift + k:shift + k + 1])
                A(H[:, k, :], NORM3[:, k, :], ACT.Identity, bias=MOD[:, shift + k:shift + k + 1]).then_inc(S("h3_ready"), 1)

        modulated(0, 0)
        act.wait_ge(S("angles_ready"), 1)
        A(ROT, ANG, ACT.Sin).then_inc(S("rot_ready"), 1)
        group_done("misc", 0)
        A(K_DS, PS[:, 0, 0:T], ACT.Copy)
        A(K_IX[:, 0, :], PS[:, 0, T:2 * T], ACT.Copy).then_inc(S("misc_copied"), 1)
        A(W_IX, PS[:, 1, :].rearrange("p (m n) -> p m n", m=2)[:, :, P:P + IDX_HEADS], ACT.Copy,
          scale=float(IDX_HEADS ** -0.5 * IDX_DIM ** -0.5))
        A(V_DS, PS[:, 1, :].rearrange("p (m n) -> p m n", m=2)[:, :, 0:P], ACT.Copy).then_inc(read_out[0], 1)

        def copied(name, j, dst):
            group_done(name, j)
            p, _n = PAIR[name, j]
            A(dst.rearrange("p c t -> p (c t)"), bank2(p), ACT.Copy).then_inc(read_out[p], 1)

        def relu(q):
            act.wait_ge(S("rel_mm"), q + 1)
            if q > 0:
                act.wait_ge(S("rel_used"), q)
            A(REL, PS[:, 4:8, 0:TRI], ACT.Relu).then_inc(S("rel_read"), 1)

        for j in range(2):
            copied("q_ix", j, Q_IX[:, 4 * j:4 * j + 4, :])
        copied("qk_sb", 0, Q_SB[:, 0:4, :])
        copied("qk_sb", 1, K_SB[:, 0:4, :])
        relu(0)
        copied("qk_sb", 2, Q_SB[:, 4:8, :])
        for q in range(1, 4):
            relu(q)
        copied("qk_sb", 3, K_SB[:, 4:8, :])
        for q in range(2):
            act.wait_ge(S("sb_mm"), 3 * q + 1)
            A(SBB[:, q, 0], PS[:, 4:8, 0:TRI], ACT.Copy, scale=float(P ** -0.5)).then_inc(S("sb_z"), 1)
            act.wait_ge(S("sb_minus"), q + 1)
            t.give(A(SBB[:, q, 1], SBB[:, q, 1], ACT.Exp), S("sb_exp"))
            act.wait_ge(S("sb_exp"), q + 1)
            A(SBB[:, q, 1], SBB[:, q, 1], ACT.Ln, bias=ones[:, 0:1]).then_inc(S("sb_log"), 1)
            group_done("v_q", 2 * q)
            p, _n = PAIR["v_q", 2 * q]
            A(V_SB[:, :, q * 512:(q + 1) * 512], PS[:, 2 * p:2 * p + 2, :], ACT.Copy).then_inc(read_out[p], 1)
            act.wait_ge(S("sb_exponent"), q + 1)
            A(SBB[:, q, 3], SBB[:, q, 3], ACT.Exp).then_inc(S("sb_weights"), 1)
            copied("v_q", 2 * q + 1, Q_DS[:, 4 * q:4 * q + 4, :])
            act.wait_ge(S("sb_mm"), 3 * q + 3)
            A(O3[:, 4 * q:4 * q + 4, :].rearrange("p c t -> p (c t)"), bank2(2), ACT.Copy).then_inc(S("sb_stored"), 1)
        act.wait_ge(S("sb_stored"), 2)
        t.give(A(SQ3[:, 0:8, :], O3[:, 0:8, :], ACT.Square), S("squared"))
        for q in range(2):
            act.wait_ge(S("ds_max"), q + 1)
            for n in range(4):
                for m in range(2):
                    k = 4 * m + n
                    ins = A(LG[:, n, m * P:m * T + P], LG[:, n, m * P:m * T + P], ACT.Exp, bias=SM3[:, k:k + 1],
                            accum_out=SM3[:, 8 + k:9 + k])
            ins.then_inc(S("ds_exp"), 1)
            act.wait_ge(S("ds_mm"), 3 * q + 2)
            A(PTR, PS[:, 4:8, 0:TRI], ACT.Copy).then_inc(S("ds_turned"), 1)
            act.wait_ge(S("ds_mm"), 3 * q + 3)
            A(O3[:, 8 + 4 * q:12 + 4 * q, :].rearrange("p c t -> p (c t)"), bank2(2), ACT.Copy).then_inc(S("ds_stored"), 1)
        act.wait_ge(S("ds_stored"), 2)
        t.give(A(SQ3[:, 8:16, :], O3[:, 8:16, :], ACT.Square), S("squared"))
        root(4, 0, 1.0 / WIDTH, 0)
        root(5, 1, 1.0 / WIDTH, 0)
        act.wait_ge(S("x3_ready"), 1)
        t.give(A(SQ3, X[:, :, :], ACT.Square), S("squared"))
        root(4, 0, 1.0 / D, 0)
        split(slot0("ffn3"), 2)
        modulated(1, 48)
        act.wait_ge(S("up_zeroed"), 1)
        with act.Fori(0, 11) as i:
            for j in range(2):
                split(slot0("ffn3", j) + 2, 4, i, 8)
                if j == 0:
                    act.wait_ge(S("hid3_full"), i + 1)
                group_done("ffn3", j, i, 8)
                A(UP3[:, 4 * j:4 * j + 4, 2:T + 2], PS[:, 2 * j:2 * j + 2, :].rearrange("p b (c t) -> p (b c) t", t=T), ACT.Copy)\
                    .then_inc(read_out[j], 1)
            act.wait_ge(S("gate_conv"), i + 1)
            A(GSIG, UC[:, 0:4, :], ACT.Sigmoid).then_inc(S("ffn_sig"), 1)
        split(slot0("down3") + 2, 4 * 11 - 2)
        act.wait_ge(S("x3_ready"), 2)
        t.give(A(SQ3, X[:, :, :], ACT.Square), S("squared"))
        root(4, 0, 1.0 / D, 0)

    @block.gpsimd
    def _(gp):
        t = Tally(gp)
        gp.memset(PADS.rearrange("p a b c -> p (a b c)"), 0.0).then_inc(S("pads_zeroed"), 1)
        def modulations(run):
            slots, sums, product = ADA[run]
            first = sum(n for _, n in ADA_RUNS[:run])
            for g in range(first, first + ADA_RUNS[run][1]):
                o = sums[:, g % ADA_SUMS, :]
                gp.wait_ge(S("ada_summed"), g + 1)
                for s in range(4):
                    n = 4 * g + s
                    gp.wait_ge(S(f"ada_loaded{n % ADA_RING}"), 16 * (n // ADA_RING + 1))
                    ws = slots[:, n % ADA_RING, :].rearrange("p (k c) -> p k c", k=KPS)
                    for k in range(KPS):
                        c = CS[:, s * KPS + k:s * KPS + k + 1]
                        first_one = s == k == 0
                        part = o if first_one else product[:, k % 2, :]
                        t.give(gp.tensor_scalar(part, ws[:, k, :], c, None, ALU.mult), S("ada_step"))
                        if not first_one:
                            gp.wait_ge(S("ada_step"), t.value(S("ada_step")))
                            t.give(gp.tensor_tensor(o, o, part, ALU.add), S("ada_step"))
                    gp.wait_ge(S("ada_step"), t.value(S("ada_step")))
                    t.give(gp.nop(), S("ada_used"))
                t.give(gp.nop(), S("ada_partial"))

        gp.wait_ge(S("const_loaded"), 32)
        gp.wait_ge(S("c_ready"), 1)
        t.give(gp.nop(), S("ada_used"), ADA_RING)
        modulations(0)
        gp.wait_ge(S("z_gated"), 4)
        gp.wait_ge(S("y_mla_ready"), HEADS)
        gp.memset(w(22528, 3584 + 2048 + 1024 + 1024 + 2048 + 256 + 256 + 256), 0.0).then_inc(S("rw_zeroed"), 1)
        gp.wait_ge(S("rw_zeroed"), 1)
        gp.nop().then_inc(S("zeros_ready"), 1)
        with gp.Fori(0, PAIRS) as i:
            gp.wait_ge(S("stage_free"), i + 1)
            gp.nop()
            for dst, src in ((RC, RR_), (KC, KK_), (NC_, NKK)):
                gp.tensor_copy(dst, src[:, bass.ds(i, 1), :].rearrange("p a t -> p (a t)"))
            gp.tensor_copy(PP, PR[:, bass.ds(PAR["pair"] + i * 8, 8)])
            gp.tensor_copy(VD, VV_[:, bass.ds(i, 1), :].rearrange("p a (c s) -> p (a c) s", s=CH).unsqueeze(2)
                           .broadcast_to([P, 4, 2, CH])).then_inc(S("staged"), 1)
            gp.wait_ge(S("const_loaded"), 32)
            gp.wait_ge(S("rb_ready"), i + 1)
            gp.tensor_copy(KK_[:, bass.ds(i, 1), :].rearrange("p a t -> p (a t)"), RB).then_inc(S("rb_stored"), 1)
            gp.wait_ge(S("rb_stored"), i + 1)
        modulations(1)
        gp.wait_ge(S("ds_stored"), 2)
        gp.wait_ge(S("x3_ready"), 1)
        gp.memset(UP3.rearrange("p a b -> p (a b)"), 0.0).then_inc(S("up_zeroed"), 1)

    @block.vector
    def _(v):
        t = Tally(v)
        tt, ts, stt = v.tensor_tensor, v.tensor_scalar, v.scalar_tensor_tensor

        def step(ins):
            t.give(ins, S("v_step"))
            v.wait_ge(S("v_step"), t.value(S("v_step")))

        def add_chunks(src, n, k):
            t.give(v.tensor_reduce(RED[:, k, :], src.rearrange("p c t -> p t c"), AX.X, ALU.add), S("red_ready"))

        def invert(k):
            t.wait(S("rooted"), 1)
            step(v.reciprocal(STD[:, k, :], STD[:, k, :]))

        def group_done(name, j, i=None, step_=0):
            n = used(name, j)
            v.wait_ge(w_used, n if i is None else n + i * step_)

        def bank2(p):
            return PS[:, 2 * p:2 * p + 2, :].rearrange("p b n -> p (b n)")

        def split(first, count, i=None, step_=0):
            for n in range(first, first + count):
                for half in range(2):
                    e = 2 * SPLIT_AT[n] + half
                    v.wait_ge(S("hi_ready"), e + 1 if i is None else e + 1 + i * 2 * step_)
                    x, lo = (r[:, n % RING, half * (SLOT // 2):(half + 1) * (SLOT // 2)] for r in (ring, ring_parts))
                    tt(lo, x, HI[:, e % 4, :].bitcast(F32), ALU.subtract).then_inc(S("lo_ready"), 1)

        t.wait(S("squared"), 1)
        add_chunks(SQ, DC, 0)
        v.wait_ge(S("c_sig"), 1)
        v.wait_ge(S("const_loaded"), 32)
        t.give(tt(CS[:, :], CS[:, :], par("c", 0, DC), ALU.mult), S("c_ready"))
        invert(0)
        for k in range(DC):
            t.give(stt(H[:, k, :], X[:, k, :], par("g_pre", k), STD[:, 0, :], ALU.mult, ALU.mult), S("h_ready"))
        t.wait(S("squared"), 1)
        add_chunks(SQ[:, 0:4, :], 4, 1)
        t.wait(S("squared"), 1)
        v.wait_ge(S("h_ready"), DC)
        add_chunks(SQ[:, 4:8, :], 4, 0)
        invert(1)
        for k in range(4):
            ins = stt(QAN[:, k, :], QA[:, k, :], par("q_norm", k), STD[:, 1, :], ALU.mult, ALU.mult)
        t.give(ins, S("latents_ready"))
        invert(0)
        for k in range(4):
            ins = stt(KVAN[:, k, :], KVA[:, k, :], par("kv_norm", k), STD[:, 0, :], ALU.mult, ALU.mult)
        t.give(ins, S("latents_ready"))
        v.wait_ge(S("kr_copied"), 1)
        v.wait_ge(S("swapped"), 1)
        step(tt(RT[:, 1, :], PS[:, 6, 0:T], con("sin", T), ALU.mult))
        t.give(tt(RT[:, 2, :], KR, con("cos", T), ALU.mult), S("kr_rotated"))
        v.wait_ge(S("kr_rotated"), 1)
        step(tt(KR2, RT[:, 1, :], RT[:, 2, :], ALU.add))

        def shift(k, mu, dst, k_sem, i=None):
            mid = PADS[:, k, :, 1:T + 1]
            step(tt(SH[:, 0, :, :], PADS[:, k, :, 0:T], PADS[:, k, :, 2:T + 2], ALU.add))
            step(stt(SH[:, 1, :, :], SH[:, 0, :, :], 0.5, mid, ALU.mult, ALU.subtract))
            for m in range(4):
                t.give(stt(dst(m), SH[:, 1, m, :], mu(m), PADS[:, k, m, 1:T + 1], ALU.mult, ALU.add), k_sem)

        v.wait_ge(read_out[PAIR["lora", 0][0]], PAIR["lora", 0][1])
        shift(1, lambda m: par("mu_lora", m), lambda m: SG1[:, m, :], S("lora_shifted"))
        v.wait_ge(S("tw_ready"), 2)
        t.give(v.nop(), S("pad_free"), 2)
        with v.Fori(0, 3) as i:
            t.enter(i, {S("v_step"): 4, S("pad_free"): 2, S("rkv_shifted"): 8})
            for j in range(2):
                p, n = PAIR["rkv", j]
                v.wait_ge(read_out[p], n + i)
                shift(j, lambda m: PR[:, bass.ds(PAR["mu_rkv"] + i * 8 + 4 * j + m, 1)],
                      lambda m: W[:, bass.ds(4096 + i * 2048 + (4 * j + m) * T, T)], S("rkv_shifted"))
                v.wait_ge(S("rkv_shifted"), t.value(S("rkv_shifted")))
                t.give(v.nop(), S("pad_free"))
            t.leave(3)

        def gate_z(name, j, k):
            v.wait_ge(S("z_sig"), k + 1)
            p, n = PAIR[name, j]
            tt(Z[:, 4 * k:4 * k + 4, :].rearrange("p c t -> p (c t)"), bank2(p), SG1.rearrange("p c t -> p (c t)"),
               ALU.mult).then_inc(read_out[p], 1)
            v.wait_ge(read_out[p], n)
            t.give(v.nop(), S("z_gated"))

        for k in range(8):
            ins = ts(NKK[:, k, :], KK_[:, k, :], par("k_k", k), -1.0, ALU.mult, ALU.mult)
        t.give(ins, S("kk_scaled"))
        for j in range(2):
            gate_z("z", j, j)
        v.wait_ge(S("kk_rooted"), 1)
        kkn = w(33344, 2048)
        step(ts(kkn, kkn, 1e-12, None, ALU.max))
        step(v.reciprocal(kkn, kkn))
        step(tt(NKK.rearrange("p c t -> p (c t)"), NKK.rearrange("p c t -> p (c t)"), kkn, ALU.mult))
        step(v.memset(QR.rearrange("p c t -> p (c t)"), 0.0))
        v.wait_ge(S("swapped"), 2)
        v.wait_ge(S("qraw_copied"), 1)
        sw = PS[:, 6:8, :].rearrange("p b (c t) -> p (b c) t", t=T)
        step(tt(RT, sw, rows(con("sin", T), 4), ALU.mult))
        step(tt(QRAW, QRAW, rows(con("cos", T), 4), ALU.mult))
        for hh in range(2):
            rr = slice(64 * hh, 64 * hh + 64)
            ins = tt(QR[rr, hh::2, :], RT[rr, :, :], QRAW[rr, :, :], ALU.add)
        t.give(ins, S("q_rotated"))
        scale = float(NOPE + ROPE) ** -0.5
        for hd in range(HEADS + 2):
            if hd < HEADS:
                k = 4 * (hd % 2)
                v.wait_ge(S("scores_ready"), hd + 1)
                step(v.tensor_reduce(SM[:, 16 + k:18 + k], PS[:, 4 + hd % 2, :].rearrange("p (a b) -> p a b", a=2), AX.X, ALU.max))
                if hd >= 2:
                    v.wait_ge(S("exp_done"), 2 * (hd - 1))
                t.give(ts(SM[:, k:k + 2], SM[:, 16 + k:18 + k], -scale, None, ALU.mult), S("max_ready"))
            if hd >= 1 and hd <= HEADS:
                g = hd - 1
                k = 4 * (g % 2)
                v.wait_ge(S("exp_done"), 2 * (g + 1))
                step(v.reciprocal(SM[:, 24 + k:26 + k], SM[:, 8 + k:10 + k]))
                for q in range(2):
                    ins = ts(PB[:, g % 2, q, :], PB[:, g % 2, q, :], SM[:, 24 + k + q:25 + k + q], None, ALU.mult)
                    if q == 1:
                        t.give(ins, S("probs_ready"))
            if hd >= 1 and hd - 1 in (3, 6):
                gate_z("z2", (hd - 1 - 3) // 3, 2 + (hd - 1 - 3) // 3)
            if hd >= 2:
                g = hd - 2
                v.wait_ge(S("pv_ready"), g + 1)
                t.give(tt(Z[:, g, :], PS[:, 7, 0:T], Z[:, g, :], ALU.mult), S("y_mla_ready"))
        t.give(v.nop(), S("pair_done"))
        t.give(v.nop(), S("stage_free"))
        v.wait_ge(S("zeros_ready"), 1)
        sm = {S(k): n for k, n in dict(staged=1, prep_sg=4, prep_cs=1, exps_ready=3, tilde_ready=1, stage_free=1,
                                       rb_ready=1, l_mm=2, gram_mm=2, l_read=2, y_init=2, gram_read=4, z_mm=10, z_ready=10,
                                       u_mm=8, u_ready=8, sa_mm=8, sa_ready=8, s_mm=6, s_ready=6, pair_done=1,
                                       v_step=V_STEPS).items()}
        lvl = lambda d, l: rows(con("lvl", P, (d * 6 + l - 1) * P), 4)
        with v.Fori(0, PAIRS) as i:
            t.enter(i, sm)
            t.wait(S("staged"), 1)
            t.wait(S("prep_sg"), 4)
            v.tensor_tensor_scan(out=CSUM[:, 0, :], data0=con("reset", T), data1=SG[:, 0, :], initial=0.0,
                                 op0=ALU.mult, op1=ALU.add)
            step(v.tensor_tensor_scan(out=CSUM[:, 1, ::-1], data0=con("reset", T), data1=SG[:, 1, ::-1], initial=0.0,
                                      op0=ALU.mult, op1=ALU.add))
            t.give(tt(EM, CSUM, SG[:, 0:2, :], ALU.subtract), S("prep_cs"))
            step(ts(TM, SG[:, 2:4, :], 1.0, PP[:, 4:5], ALU.subtract, ALU.mult))
            step(stt(KD, TM, 1.0, rows(KC, 2), ALU.add, ALU.mult))
            step(stt(BD, SG[:, 2:4, :], -1.0, rows(NC_, 2), ALU.mult, ALU.mult))
            step(tt(TM[:, 0, :], KD[:, 0, :], KD[:, 1, :], ALU.add))
            t.give(stt(RB, TM[:, 0, :], PP[:, 5:6], RC, ALU.mult, ALU.mult), S("rb_ready"))
            t.wait(S("exps_ready"), 3)
            e8 = lambda x: x.rearrange("p d (c s) -> p (d c) s", s=CH)
            d2 = lambda x: x.rearrange("p (d c) s -> p d c s", d=2)
            for hh in range(2):
                rr = slice(64 * hh, 64 * hh + 64)
                tt(BK[rr, :, 3 * hh, :], e8(BD[rr]), e8(EN[rr]), ALU.mult)
                tt(BK[rr, :, 1 + hh, :], e8(KD[rr]), e8(EN[rr]), ALU.mult)
                for d in range(2):
                    tt(AR[rr, 4 * d:4 * d + 4, hh, :], NC_[rr].rearrange("p (c s) -> p c s", s=CH),
                       EM[rr, d].rearrange("p (c s) -> p c s", s=CH), ALU.mult)
            for d in range(2):
                ins = tt(AR[:, 4 * d:4 * d + 4, 2, :], RC.rearrange("p (c s) -> p c s", s=CH),
                         EP[:, d].rearrange("p (c s) -> p c s", s=CH), ALU.mult)
            t.give(ins, S("tilde_ready"))
            v.wait_ge(S("tilde_ready"), t.value(S("tilde_ready")))
            t.give(v.nop(), S("stage_free"))
            for d in range(2):
                t.wait(S("l_mm"), 1)
                lm = rows(con("lmask", P, d * P), 4)
                t.give(tt(LS[:, d], PS[:, 4, :].rearrange("p (c n) -> p c n", c=4), lm, ALU.mult), S("l_read"))
                v.wait_ge(S("l_read"), t.value(S("l_read")))
                step(tt(XY[:, d, 1], LS[:, d], lvl(1 - d, 1), ALU.mult))
                t.give(tt(XY[:, d, 1], XY[:, d, 1], rows(ident, 4), ALU.add), S("y_init"))
                t.wait(S("gram_mm"), 1)
                g0 = PS[:, 2, :].rearrange("p (c n) -> p c n", c=4)
                g1 = PS[:, 3, :].rearrange("p (c n) -> p c n", c=4)
                st_, inc = con("strict", CH, d * CH), con("incl", CH, d * CH)
                tt(AK[64:128, 4 * d:4 * d + 4, 0:CH], g0[64:128, :, 0:CH], rows(st_[64:128], 4), ALU.mult)
                t.give(tt(RRM[:, d, 0], g0[:, :, CH:P], rows(inc, 4), ALU.mult), S("gram_read"))
                tt(AK[0:64, 4 * d:4 * d + 4, CH:P], g1[0:64, :, 0:CH], rows(st_[0:64], 4), ALU.mult)
                t.give(tt(RRM[:, d, 1], g1[:, :, CH:P], rows(inc, 4), ALU.mult), S("gram_read"))
            for l in range(2, 7):
                for d in range(2):
                    t.wait(S("z_mm"), 1)
                    step(tt(ZS[:, d], PS[:, 2 + 3 * d, :].rearrange("p (c n) -> p c n", c=4), lvl(d, l), ALU.mult))
                    t.give(tt(ZS[:, d], ZS[:, d], rows(ident, 4), ALU.add), S("z_ready"))
            for k in range(4):
                for d in range(2):
                    t.wait(S("u_mm"), 1)
                    t.give(v.tensor_copy(US[:, d, :], PS[:, 3 + d, 0:CH]), S("u_ready"))
                for d in range(2):
                    e = 4 * d + (k if d == 0 else 3 - k)
                    t.wait(S("sa_mm"), 1)
                    v.tensor_copy(SV[0:64, e, 0, 0:CH], PS[0:64, 3 + d, CH:P])
                    t.give(v.tensor_copy(SV[64:128, e, 1, CH:P], PS[64:128, 3 + d, CH:P]), S("sa_ready"))
                if k == 3:
                    v.wait_ge(S("sa_ready"), t.value(S("sa_ready")))
                    t.give(v.nop(), S("pair_done"))
                    continue
                for d in range(2):
                    c = k if d == 0 else 3 - k
                    pc = EP[:, d, c * CH + (CH - 1 if d == 0 else 0):c * CH + (CH - 1 if d == 0 else 0) + 1]
                    t.wait(S("s_mm"), 1)
                    s_new = PS[:, 3 + d, 2 * CH:3 * CH]
                    if k > 0:
                        step(tt(STMP[:, d], s_new, ST[:, d], ALU.add))
                        s_new = STMP[:, d]
                    ts(ST[:, d], s_new, pc, None, ALU.mult)
                    ts(SBD[0:64, d, 0:CH], s_new[0:64], pc[0:64], None, ALU.mult)
                    t.give(ts(SBD[64:128, d, CH:P], s_new[64:128], pc[64:128], None, ALU.mult), S("s_ready"))
            t.leave(PAIRS)
        yf, kf, vf = (x.rearrange("p c t -> p (c t)") for x in (RR_, KK_, VV_))
        sums = PS[:, 4:8, :].rearrange("p b n -> p (b n)")
        v.wait_ge(S("gn_mm"), 1)
        v.wait_ge(S("rb_stored"), PAIRS)
        stt(yf, sums, -1.0 / CH, yf, ALU.mult, ALU.add).then_inc(S("gn_centred"), 1)
        v.wait_ge(S("gn_rooted"), 1)
        v.wait_ge(S("gn_centred"), 1)
        sd = w(33344, 2048)
        step(v.reciprocal(sd, sd))
        step(tt(yf, yf, sd, ALU.mult))
        for k in range(8):
            ins = ts(RR_[:, k, :], RR_[:, k, :], par("gn_g", k), par("gn_b", k), ALU.mult, ALU.add)
        step(ins)
        v.wait_ge(S("gn_mm"), 3)
        step(tt(sd, sums, vf, ALU.mult))
        step(tt(yf, yf, sd, ALU.add))
        zr = Z[:, 8:16, :].rearrange("p c t -> p (c t)")
        tt(zr, zr, yf, ALU.mult).then_inc(S("y_rwkv_ready"), 1)
        for j in range(4):
            group_done("br_mla", j)
            p, n = PAIR["br_mla", j]
            tt(M1[:, 4 * j:4 * j + 4, :].rearrange("p c t -> p (c t)"), bank2(p),
               G[:, 4 * j:4 * j + 4, :].rearrange("p c t -> p (c t)"), ALU.mult).then_inc(read_out[p], 1)
        for j in range(4):
            group_done("br_rwkv", j)
            p, n = PAIR["br_rwkv", j]
            sh = SH[:, j % 2].rearrange("p c t -> p (c t)")
            tt(sh, bank2(p), G[:, 16 + 4 * j:20 + 4 * j, :].rearrange("p c t -> p (c t)"), ALU.mult).then_inc(read_out[p], 1)
            v.wait_ge(read_out[p], n)
            m = M1[:, 4 * j:4 * j + 4, :].rearrange("p c t -> p (c t)")
            ins = tt(m, m, sh, ALU.add)
        ins.then_inc(S("merged_ready"), 1)
        t.wait(S("squared"), 1)
        add_chunks(SQ, DC, 0)
        invert(0)
        v.wait_ge(S("x_loaded"), 32)
        for k in range(DC):
            ins = stt(O1[:, k, :], O1[:, k, :], par("g_post", k), STD[:, 0, :], ALU.mult, ALU.mult)
        step(ins)
        ins = tt(X[:, :, :], X[:, :, :], O1, ALU.add)
        t.give(ins, S("x_ready"))
        def centre(src, n, k):
            add_chunks(src, n, k)
            t.wait(S("rooted"), 1)
            t.give(tt(src, src, rows(STD[:, k, :], n), ALU.subtract), S("centred"))

        v.wait_ge(S("par2_loaded"), 64)
        step(v.memset(UPAD.rearrange("p a b -> p (a b)"), 0.0))
        for j in range(2):
            group_done("conv_in", 2 * j + 1)
            v.wait_ge(read_out[0], PAIR["conv_in", 2 * j][1])
            for m in range(4):
                ins = stt(UPAD[:, 4 * j + m, 15:15 + T], PS[:, 2 + m // 2, (m % 2) * T:(m % 2 + 1) * T],
                          par("b_in", 4 * j + m), SGB[:, m, :], ALU.add, ALU.mult)
            ins.then_inc(read_out[1], 1)
            v.wait_ge(read_out[1], PAIR["conv_in", 2 * j + 1][1])
            t.give(v.nop(), S("conv_u_ready"))
        v.wait_ge(S("pool_mm"), 1)
        for g in range(4):
            ins = ts(MIX[:, 8 + g, :], PS[:, 6 + g // 2, (g % 2) * T:(g % 2 + 1) * T], par("b_pool", g), par("s_pool", g),
                     ALU.add, ALU.mult)
        t.give(ins, S("pool_done"))
        group_done("four_w", 0)
        for g in range(4):
            ins = ts(MIX[:, 12 + g, :], PS[:, 6 + g // 2, (g % 2) * T:(g % 2 + 1) * T], par("b_four", g), None, ALU.add)
        t.give(ins, S("v_step"))
        for c in range(8):
            t.give(ts(ACC[:, c, :], UPAD[:, c, 0:T], par("taps", c), par("b_dw", c), ALU.mult, ALU.add), S("conv_step"))
        with v.Fori(0, TAPS - 1) as i:
            for c in range(8):
                v.wait_ge(S("conv_step"), i * 8 + c + 1)
                stt(ACC[:, c, :], W[:, bass.ds(i + (c * (T + TAPS - 1) + 1), T)], PR[:, bass.ds(i * 8 + (PAR["taps"] + 8 + c), 1)],
                    ACC[:, c, :], ALU.mult, ALU.add).then_inc(S("conv_step"), 1)
        v.wait_ge(S("conv_step"), 8 * TAPS)
        centre(ACC, 8, 0)
        t.wait(S("squared"), 1)
        add_chunks(SQ2[:, 0:8, :], 8, 1)
        invert(1)
        for k in range(8):
            t.give(stt(SQ2[:, k, :], ACC[:, k, :], par("cln_g", k), STD[:, 1, :], ALU.mult, ALU.mult), S("v_ready"))
        for k in range(8):
            v.wait_ge(S("v_sig"), k + 1)
            ins = stt(MIX[:, k, :], SQ2[:, k, :], par("cln_b", k), SQ2[:, 8 + k, :], ALU.add, ALU.mult)
        t.give(ins, S("mix_ready"))
        for j in range(4):
            p, n = PAIR["w_out2", j]
            v.wait_ge(read_out[p], n)
            ins = stt(PRE[:, 4 * j:4 * j + 4, :], X[:, 4 * j:4 * j + 4, :], ALPHA, PRE[:, 4 * j:4 * j + 4, :], ALU.mult, ALU.add)
        step(ins)

        def layer_norm(g, pre):
            centre(pre, DC, 0)
            t.wait(S("squared"), 1)
            add_chunks(SQ2, DC, 1)
            invert(1)
            for k in range(DC):
                t.give(stt(pre[:, k, :], pre[:, k, :], par(g, k), STD[:, 1, :], ALU.mult, ALU.mult), S("scaled"))

        flat = lambda x: x.rearrange("p c t -> p (c t)")
        layer_norm("ln1_g", PRE)
        v.wait_ge(S("ada_read"), 3)
        t.give(tt(MOD[:, :], MOD[:, :], par("b_ada", 0, 96), ALU.add), S("mod_ready"))
        v.wait_ge(S("p_hi"), 1)
        tt(P2_LO, P2, P2_HI.bitcast(F32), ALU.subtract)
        split(slot0("ffn2"), 2)
        v.wait_ge(S("x1_ready"), DC)
        t.give(tt(X_LO, X[:, :, :], X_HI.bitcast(F32), ALU.subtract), S("split_done"))
        t.give(v.nop(), S("hid_ready"))
        with v.Fori(0, 11) as i:
            t.enter(i, {S("v_step"): 1, S("hid_ready"): 1})
            split(slot0("ffn2", 0) + 2, 4, i, 8)
            v.wait_ge(S("ffn_sig"), i + 1)
            tt(flat(GU2), bank2(0), flat(GU), ALU.mult).then_inc(read_out[0], 1)
            split(slot0("ffn2", 1) + 2, 4, i, 8)
            group_done("ffn2", 1, i, 8)
            v.wait_ge(read_out[0], i + PAIR["ffn2", 0][1])
            tt(flat(GU3), bank2(1), flat(GU2), ALU.mult).then_inc(read_out[1], 1)
            v.wait_ge(read_out[1], i + PAIR["ffn2", 1][1])
            hh, hl = (x[:, bass.ds(i * 4, 4), :].rearrange("p c t -> p (c t)") for x in (HID_HI, HID_LO))
            step(v.tensor_copy(hh, flat(GU3)))
            t.give(tt(hl, flat(GU3), hh.bitcast(F32), ALU.subtract), S("hid_ready"))
            t.leave(11)
        t.give(v.nop(), S("ple_read"))

        def ple(i, ahead):
            split(slot0("down2") + 2, 14, i, 16)
            split(slot0("down2") + 16, ahead, i, 16)
            v.wait_ge(w_used, i * 16 + slot0("down2") + 16)
            v.wait_ge(read_out[1], i + PAIR["ple_gate", 0][1])
            tt(flat(GU2), bank2(2), flat(GU), ALU.mult).then_inc(S("ple_read"), 1)
            v.wait_ge(S("ple_read"), i + 2)
            tt(flat(GU3), bank2(0), flat(GU2), ALU.add).then_inc(read_out[0], 1)
            v.wait_ge(read_out[0], i + PAIR["down2", 0][1])
            x = X[:, bass.ds(i * 4, 4), :].rearrange("p c t -> p (c t)")
            stt(x, x, ALPHA, flat(GU3), ALU.mult, ALU.add).then_inc(S("pre_ready"), 1)

        with v.Fori(0, 3) as i:
            ple(i, 2)
        ple(3, 0)
        v.wait_ge(S("pre_ready"), 4)
        layer_norm("ln2_g", X[:, :, :])
        v.wait_ge(S("x1_ready"), 2 * DC)
        for gain, at_ in (("n1_g", 16), ("n2_g", 64)):
            if gain == "n1_g":
                v.wait_ge(S("par3_loaded"), 32)
                v.wait_ge(S("mod_ready"), 1)
            ins = stt(MOD[:, at_:at_ + DC], MOD[:, at_:at_ + DC], 1.0, par(gain, 0, DC), ALU.add, ALU.mult)
        step(ins)

        def scaled_norm(at_):
            t.wait(S("squared"), 1)
            add_chunks(SQ3, DC, 0)
            invert(0)
            for k in range(DC):
                t.give(stt(NORM3[:, k, :], X[:, k, :], MOD[:, at_ + k:at_ + k + 1], STD[:, 0, :], ALU.mult, ALU.mult), S("scaled"))

        scaled_norm(16)
        step(v.tensor_copy(TURN[:, 3, :], TURNI[:, 0, :]))
        for k in range(4):
            ins = ts(ANG[:, k, :], TURN[:, 3, :], con("freq", 1, 2 * (k // 2)), None, ALU.mult)
        step(ins)
        for k in range(4):
            ins = ts(TURN[:, k, :], ANG[:, k, :], float(1 / (2 * np.pi)), 0.25 * (1 - k % 2), ALU.mult, ALU.add)
        step(ins)
        step(ts(TURN, TURN, MAGIC, None, ALU.add))
        step(ts(TURN, TURN, MAGIC, None, ALU.subtract))
        for part in TWO_PI:
            step(stt(ANG, TURN, -part, ANG, ALU.mult, ALU.add))
        for k in (0, 2):
            ins = ts(ANG[:, k, :], ANG[:, k, :], float(np.pi / 2), None, ALU.add)
        step(ins)
        t.give(ts(ANG, ANG, PI_BELOW, -PI_BELOW, ALU.min, ALU.max), S("angles_ready"))
        v.wait_ge(S("rot_ready"), 1)
        for k in (1, 3):
            ins = ts(ROT[:, k, :], ROT[:, k, :], con("freq", 1, k), None, ALU.mult)
        step(ins)

        def rotate(dst, n, bank, k, src=None):
            src = dst if src is None else src
            sw = PS[:, bank:bank + (n + 1) // 2, :].rearrange("p b (c t) -> p (b c) t", t=T)[:, 0:n, :]
            t.give(tt(TURN[:, 0:n, :], sw, rows(ROT[:, k + 1, :], n), ALU.mult), S("turn_part"))
            step(tt(src, src, rows(ROT[:, k, :], n), ALU.mult))
            v.wait_ge(S("turn_part"), t.value(S("turn_part")))
            return tt(dst, src, TURN[:, 0:n, :], ALU.add)

        v.wait_ge(S("turned"), 1)
        step(rotate(K_DS.unsqueeze(1), 1, 4, 0))
        step(rotate(K_IX[:, 0:1, :], 1, 5, 2))
        step(v.tensor_copy(K_IX[64:128, 1, :], K_IX[64:128, 0, :]))
        step(v.memset(K_IX[0:64, 1, :], 0.0))
        t.give(v.memset(K_IX[64:128, 0, :], 0.0), S("turn_done"))
        v.wait_ge(S("turn_part"), t.value(S("turn_part")))
        t.give(v.nop(), S("turn_read"))
        for j in range(2):
            v.wait_ge(S("turned"), j + 2)
            t.give(rotate(Q_IX[:, 4 * j:4 * j + 4, :], 4, 6, 2), S("turn_done"))
            v.wait_ge(S("turn_done"), t.value(S("turn_done")))
            t.give(v.nop(), S("turn_read"))
        step(v.memset(SCORE, 0.0))
        for q in range(4):
            v.wait_ge(S("rel_read"), q + 1)
            for n in range(4):
                for m in range(2):
                    o = SCORE[:, m * P:m * T + P]
                    ins = stt(o, REL[:, n, m * P:m * T + P], W_IX[:, m, 4 * q + n:4 * q + n + 1], o, ALU.mult, ALU.add)
                step(ins)
            t.give(v.nop(), S("rel_used"))
        step(tt(SCORE, SCORE, con("causal", TRI), ALU.mult))
        step(tt(SCORE, SCORE, con("cneg", TRI), ALU.add))
        for m in range(2):
            src = SCORE[:, m * P:m * T + P]
            dst = LEFT[:, m * P:m * T + P]
            for k in range(TOPK // 8):
                step(v.max(TOP, src))
                step(v.match_replace(dst, TOP, src, TAKEN))
                src = dst
        step(ts(LEFT, LEFT, TAKEN, None, ALU.is_equal))
        step(tt(LEFT, LEFT, con("causal", TRI), ALU.mult))
        step(ts(SBIAS, LEFT, 1.0, -NEG, ALU.subtract, ALU.mult))
        for q in range(2):
            z, e, sp, wt = (SBB[:, q, k] for k in range(4))
            v.wait_ge(S("sb_z"), q + 1)
            t.give(stt(e, z, -1.0, z, ALU.mult, ALU.min), S("sb_minus"))
            v.wait_ge(S("sb_log"), q + 1)
            step(stt(sp, z, 0.0, e, ALU.max, ALU.add))
            t.give(tt(sp, sp, rows(con("sp_mask", TRI), 4), ALU.mult), S("sb_softplus"))
            v.wait_ge(S("sb_mm"), 3 * q + 2)
            step(tt(wt, z, PS[:, 4:8, 0:TRI], ALU.subtract))
            t.give(tt(wt, wt, rows(con("sp_min", TRI), 4), ALU.min), S("sb_exponent"))
        for j in range(2):
            v.wait_ge(S("turned"), 4 + j)
            t.give(rotate(Q_DS[:, 4 * j:4 * j + 4, :], 4, 6, 0), S("turn_done"))
            v.wait_ge(S("turn_done"), t.value(S("turn_done")))
            t.give(v.nop(), S("turn_read"))
        for q in range(2):
            v.wait_ge(S("ds_mm"), 3 * q + 1)
            step(stt(LG, PS[:, 4:8, 0:TRI], float(P ** -0.5), rows(SBIAS, 4), ALU.mult, ALU.add))
            for m in range(2):
                ins = v.tensor_reduce(SM3[:, 16 + 4 * m:20 + 4 * m], LG[:, :, m * P:m * T + P], AX.X, ALU.max)
            step(ins)
            t.give(ts(SM3[:, 0:8], SM3[:, 16:24], -1.0, None, ALU.mult), S("ds_max"))
            v.wait_ge(S("ds_exp"), q + 1)
            step(v.reciprocal(SM3[:, 24:32], SM3[:, 8:16]))
            for m in range(2):
                o = LG[:, :, m * P:m * T + P]
                ins = tt(o, o, SM3[:, 24 + 4 * m:28 + 4 * m].unsqueeze(2).broadcast_to([P, 4, P + m * P]), ALU.mult)
            t.give(ins, S("ds_probs"))
        for k in range(2):
            t.wait(S("squared"), 1)
            add_chunks(SQ3[:, 8 * k:8 * k + 8, :], 8, k)
        for k, gain in enumerate(("sb_g", "ds_g")):
            invert(k)
            for m in range(8):
                c = 8 * k + m
                ins = stt(O3[:, c, :], O3[:, c, :], par(gain, m), STD[:, k, :], ALU.mult, ALU.mult)
            t.give(ins, S("o3_ready"))

        def gated_residual(name, gate, ahead=0):
            for j in range(4):
                if ahead:
                    split(slot0(name, j) + 11, (11, 11, 11, 0)[j])
                group_done(name, j)
                p, _n = PAIR[name, j]
                for m in range(4):
                    c = 4 * j + m
                    ins = stt(X[:, c, :], PS[:, 2 * p + m // 2, (m % 2) * T:(m % 2 + 1) * T],
                              MOD[:, gate + c:gate + c + 1], X[:, c, :], ALU.mult, ALU.add)
                ins.then_inc(read_out[p], 1)
            for j in range(2, 4):
                v.wait_ge(read_out[PAIR[name, j][0]], PAIR[name, j][1])
            t.give(v.nop(), S("x3_ready"))

        gated_residual("w_out3", 32)
        scaled_norm(64)
        split(slot0("ffn3"), 2)
        v.wait_ge(S("h3_ready"), 2 * DC)
        t.give(tt(H3_LO, H, H3_HI.bitcast(F32), ALU.subtract), S("split_done"))
        t.give(v.nop(), S("hid3_full"))
        with v.Fori(0, 11) as i:
            t.enter(i, {S("v_step"): 6, S("up_used"): 1, S("gate_conv"): 1, S("hid3_full"): 1, S("hid_ready"): 1})
            for j in range(2):
                split(slot0("ffn3", j) + 2, 4, i, 8)
                v.wait_ge(read_out[j], i + PAIR["ffn3", j][1])
                col = lambda m, tap: PR[:, bass.ds(PAR["conv_w"] + 3 * (FF3_CHUNKS * j + m) + tap + i * 12, 1)]
                for m in range(4):
                    c = 4 * j + m
                    ins = ts(UC[:, c, :], UP3[:, c, 0:T], col(m, 0),
                             PR[:, bass.ds(PAR["conv_b"] + FF3_CHUNKS * j + m + i * 4, 1)], ALU.mult, ALU.add)
                step(ins)
                for tap in (1, 2):
                    for m in range(4):
                        c = 4 * j + m
                        ins = stt(UC[:, c, :], UP3[:, c, tap:tap + T], col(m, tap), UC[:, c, :], ALU.mult, ALU.add)
                    if tap == 1:
                        step(ins)
                t.give(ins, S("gate_conv") if j == 0 else S("up_used"))
            v.wait_ge(S("ffn_sig"), i + 12)
            step(tt(UC[:, 0:4, :], UC[:, 0:4, :], GSIG, ALU.mult))
            v.wait_ge(S("up_used"), i + 1)
            t.give(tt(UC[:, 4:8, :], UC[:, 4:8, :], UC[:, 0:4, :], ALU.mult), S("hid3_full"))
            v.wait_ge(S("hid3_full"), i + 2)
            hh, hl = (x[:, bass.ds(i * 4, 4), :].rearrange("p c t -> p (c t)") for x in (HID3_HI, HID3_LO))
            step(v.tensor_copy(hh, flat(UC[:, 4:8, :])))
            t.give(tt(hl, flat(UC[:, 4:8, :]), hh.bitcast(F32), ALU.subtract), S("hid_ready"))
            v.wait_ge(S("hid_ready"), i + 13)
            t.leave(11)
        split(slot0("down3") + 2, 9)
        gated_residual("down3", 80, 11)
        t.wait(S("squared"), 1)
        add_chunks(SQ3, DC, 0)
        invert(0)
        for k in range(DC):
            ins = stt(OUT[:, k, :], X[:, k, :], par("fin_g", k), STD[:, 0, :], ALU.mult, ALU.mult)
            if k % 4 == 3:
                t.give(ins, S("out_ready"))


def packed(x, width=COLS):
    K, N = x.shape
    kps = SLOT // width
    n = -(-K // (P * kps))
    out = np.zeros((n * kps * P, width), x.dtype)
    out[:K, :N] = x
    return out.reshape(n, kps, P, width).transpose(0, 2, 1, 3).reshape(n, P, SLOT)


def columns(x, chunks=None):
    x = np.asarray(x).reshape(-1, P).T
    if chunks is not None and x.shape[1] < chunks:
        x = np.concatenate([x, np.zeros((P, chunks - x.shape[1]), x.dtype)], 1)
    return x


def fm(x):
    return np.ascontiguousarray(x.T.reshape(-1, P, x.shape[0]).transpose(1, 0, 2))


def padded_rank(x):
    out = np.zeros((x.shape[0], 4 * P), x.dtype)
    for m in range(4):
        out[:, m * P:m * P + LORA] = x[:, m * LORA:(m + 1) * LORA]
    return out


def weight_slots(g):
    out = {}

    def groups(name, x, width=COLS):
        out.setdefault(name, []).extend(packed(x[:, c:c + width]) for c in range(0, x.shape[1], width))

    w_in = g["w_in"]
    o = 2 * RANK + ROPE
    groups("qa", w_in[:, 0:RANK])
    groups("kva", w_in[:, RANK:2 * RANK])
    kr = w_in[:, 2 * RANK:o]
    out["kr"] = [packed(np.concatenate([kr, kr], 1), P)]
    groups("rkv", w_in[:, o:o + 3 * WIDTH])
    o += 3 * WIDTH
    groups("lora", padded_rank(w_in[:, o:o + 4 * LORA]))
    o += 4 * LORA
    groups("z", w_in[:, o:o + WIDTH])
    groups("z2", w_in[:, o + WIDTH:o + 2 * WIDTH])
    groups("gates", w_in[:, o + 2 * WIDTH:])
    q = g["mla_wq_b"].reshape(RANK, HEADS, NOPE + ROPE)
    groups("q_nope", q[:, :, :NOPE].reshape(RANK, -1))
    groups("q_rope", q[:, :, NOPE:].reshape(RANK, -1))
    kv = g["mla_wkv_b"].reshape(RANK, HEADS, 2 * NOPE)
    groups("k_nope", kv[:, :, :NOPE].reshape(RANK, -1))
    groups("v_mla", kv[:, :, NOPE:].reshape(RANK, -1))
    groups("br_mla", g["w_br_mla"])
    groups("br_rwkv", g["w_br_rwkv"])
    groups("w_out", g["w_out"])
    w2 = g["w_in_2"][0]
    for j in range(2):
        groups("conv_in", w2[:, 1024 + 512 * j:1536 + 512 * j])
        groups("conv_in", w2[:, 512 * j:512 * j + 512])
    groups("pool_in", w2[:, 2048:2560])
    groups("four_in", w2[:, 2560:])
    pool, dft, feat = seq_matrices()
    out["poolmat"] = [pool[None]]
    wp = g["w_pool_2"][0].transpose(1, 0, 2).reshape(P, 512)
    out["seqmat"] = [np.concatenate([wp, dft, feat, np.zeros((P, 256), np.float32)], 1)[None]]
    wf = g["w_fourier_2"][0].transpose(1, 0, 2).reshape(P, 512)
    out["four_w"] = [np.concatenate([wf, np.zeros((P, 1536), np.float32)], 1)[None]]
    groups("w_out2", g["w_out_2"][0])
    for j in range(11):
        groups("ffn2", g["w_gate_2"][0][:, 512 * j:512 * j + 512])
        groups("ffn2", g["w_up_2"][0][:, 512 * j:512 * j + 512])
    for j in range(4):
        for nm in ("w_down_2", "w_ple_gate_2"):
            groups("down2", g[nm][0][:, 512 * j:512 * j + 512])
        ple = g["w_ple_2"][0][:, 512 * j:512 * j + 512]
        gap = np.zeros((P, 512), ple.dtype)
        groups("down2", np.concatenate([ple[:P], gap, ple[P:], gap], 0))
    w3 = g["w_in_3"][0]
    shared = np.zeros((D, 4 * P), w3.dtype)
    shared[:, 0:P], shared[:, P:2 * P] = w3[:, 4096:4224], w3[:, 4224:4352]
    shared[:, 2 * P:2 * P + 64] = shared[:, 2 * P + 64:3 * P] = w3[:, 5376:5440]
    shared[:, 3 * P:3 * P + IDX_HEADS] = w3[:, 5440:5456]
    groups("misc", shared)
    groups("q_ix", w3[:, 4352:5376])
    for c in (0, 1024, 512, 1536):
        groups("qk_sb", w3[:, c:c + 512])
    for c in (2048, 3072, 2560, 3584):
        groups("v_q", w3[:, c:c + 512])
    groups("w_out3", g["w_out_3"][0])
    for j in range(11):
        for c in (0, FF3):
            groups("ffn3", g["w_up_3"][0][:, c + 512 * j:c + min(512 * j + 512, FF3)])
    groups("down3", g["w_down_3"][0])
    slots = [s for name, _, _ in STREAM for part in out[name] for s in part]
    return np.stack(slots)


def ada_slots(g):
    x = g["w_ada_3"][0]
    return np.concatenate([packed(x[:, c:c + COLS]) for c in range(0, x.shape[1], COLS)])


def params(g):
    o = 3 * WIDTH
    z = np.zeros
    pair = np.zeros((P, PAIRS, PAIR_PARAMS), np.float32)
    for k, name in enumerate(("rwkv_w0_f", "rwkv_w0_b", "rwkv_a0_f", "rwkv_a0_b", "rwkv_k_a", "rwkv_r_k")):
        pair[:, :, k] = columns(g[name].reshape(-1))
    mu = g["rwkv_mu"]
    part = {
        "g_pre": columns(g["g_pre"]), "q_norm": columns(g["mla_q_norm"]), "kv_norm": columns(g["mla_kv_norm"]),
        "mu_lora": columns(padded_rank(mu[None, o:])), "mu_rkv": columns(mu[:o]), "pair": pair.reshape(P, -1),
        "k_k": columns(g["rwkv_k_k"]), "gn_g": columns(g["rwkv_gn_g"]), "gn_b": columns(g["rwkv_gn_b"]),
        "g_post": columns(g["g_post"]), "c": columns(g["c_3"]),
    }
    g2 = {n[:-2]: x[0] for n, x in g.items() if n.endswith("_2")}
    part.update({
        "b_in": columns(g2["b_in"]), "taps": g2["w_dw"].reshape(TAPS, 8, P).transpose(2, 0, 1).reshape(P, -1),
        "b_dw": columns(g2["b_dw"]), "cln_g": columns(g2["conv_ln_g"]), "cln_b": columns(g2["conv_ln_b"]),
        "b_pool": columns(g2["b_pool"]), "s_pool": columns(g2["pool_scale"]), "b_four": columns(g2["b_fourier"]),
        "b_out": columns(g2["b_out"]), "ln1_g": columns(g2["ln1_g"]), "ln1_b": columns(g2["ln1_b"]),
        "ln2_g": columns(g2["ln2_g"]), "ln2_b": columns(g2["ln2_b"]),
        "b_ada": columns(g["b_ada_3"][0]),
    })
    two = lambda x: np.concatenate([columns(x[:FF3], FF3_CHUNKS), columns(x[FF3:], FF3_CHUNKS)], 1)
    part.update({
        "n1_g": columns(g["norm1_g_3"]), "sb_g": columns(g["sb_norm_g_3"]), "ds_g": columns(g["dsa_norm_g_3"]),
        "n2_g": columns(g["norm2_g_3"]), "fin_g": columns(g["final_norm_g_3"]), "conv_b": two(g["conv_b_3"][0]),
        "conv_w": np.stack([two(g["conv_w_3"][0, k]) for k in range(3)], 2).reshape(P, -1),
    })
    return [np.ascontiguousarray(np.concatenate([part[n] for n, _ in b], 1)) for b in PARAMS]


def seq_matrices():
    s = np.arange(T)
    pool = np.zeros((T, 4, T))
    for g, k in enumerate(POOL_WINDOWS):
        lo, hi = np.clip(s - k // 2, 0, T), np.clip(s + k // 2, 0, T)
        inside = (s[:, None] >= lo[None, :]) & (s[:, None] < hi[None, :])
        pool[:, g, :] = inside / (hi - lo)[None, :] - np.eye(T)
    tok = 2 * np.pi * ((s[:, None] * s[None, :]) % T) / T
    dft = np.concatenate([np.cos(tok), np.sin(tok)], 1) / np.sqrt(T)
    c = np.arange(P)
    ang = 2 * np.pi * ((c[:, None] * c[None, :]) % P) / P
    feat = np.concatenate([np.cos(ang), -np.sin(ang)], 1) / np.sqrt(P)
    two = lambda x: x.reshape(2, P, -1).transpose(1, 0, 2).reshape(P, -1).astype(np.float32)
    return two(pool.reshape(T, -1)), two(dft), feat.astype(np.float32)


def constants():
    f = np.float32
    r = np.arange(P)
    s64 = r % CH
    same = (r[:, None] // CH) == (r[None, :] // CH)
    com = {"ident": np.eye(P), "ones": np.ones((P, P)), "eps": np.tile([EPS, EPS_GN, EPS_LN, 0.0], (P, 1))}
    swap = np.zeros((P, P))
    swap[(r // CH) * CH + (s64 + 32) % CH, r] = 1.0
    pos = np.arange(T, dtype=f)
    inv = np.power(f(10000.0), -np.arange(0, ROPE, 2, dtype=f) / f(ROPE)).astype(f)
    ang = (inv[:, None] * pos[None, :]).astype(f)
    cos, sin = np.cos(ang), np.sin(ang)
    lvl = []
    for d in range(2):
        for l in range(1, 7):
            i, j = (s64[:, None], s64[None, :]) if d == 0 else (s64[None, :], s64[:, None])
            lvl.append(same & (i >> l == j >> l) & ((i >> (l - 1)) % 2 == 0) & ((j >> (l - 1)) % 2 == 1))
    t64 = np.arange(CH)
    a, b = s64[:, None], t64[None, :]
    one = {
        "bones": same, "swap": swap, "cos": np.tile(cos, (4, 1)), "sin": np.tile(np.concatenate([-sin, sin]), (2, 1)),
        "reset": np.tile((np.arange(T) % CH != 0), (P, 1)), "lvl": np.concatenate(lvl, 1),
        "strict": np.concatenate([a < b, a > b], 1), "incl": np.concatenate([a <= b, a >= b], 1),
        "lmask": np.concatenate([same & (s64[:, None] > s64[None, :]), same & (s64[:, None] < s64[None, :])], 1),
    }
    c1 = np.concatenate([np.asarray({**com, **one}[n], f) for n, _ in C_ALL + C_1], 1)
    f32 = f
    three = {}
    swap128 = np.eye(P)
    swap128[:32, :32] = 0.0
    swap128[(r[:32] + 16) % 32, r[:32]] = 1.0
    swap64 = np.eye(P)
    for hh in (0, 64):
        swap64[hh:hh + 16, hh:hh + 16] = 0.0
        swap64[hh + (r[:16] + 8) % 16, hh + r[:16]] = 1.0
    three["swap128"], three["swap64"] = swap128, swap64
    three["tri"] = r[:, None] >= r[None, :]
    t0, t1 = np.arange(T), np.arange(P)
    strict = np.concatenate([r[:, None] < t0[None, :], r[:, None] < t1[None, :]], 1)
    three["sp_mask"], three["sp_min"] = strict, np.where(strict, 0.0, NEG)
    causal = np.concatenate([r[:, None] >= t1[None, :], r[:, None] + P >= t0[None, :]], 1)
    three["causal"], three["cneg"] = causal, np.where(causal, 0.0, NEG)
    f128 = np.zeros(P)
    f128[:32] = np.tile(np.power(f32(500000.0), -np.arange(16, dtype=f32) / f32(16)), 2)
    f64 = np.zeros(P)
    for hh in (0, 64):
        f64[hh:hh + 16] = np.tile(np.power(f32(500000.0), -np.arange(8, dtype=f32) / f32(8)), 2)
    sign = lambda x, n: np.where((x > 0) & (r % (64 if n == 8 else 128) < n), -1.0, 1.0)
    three["freq"] = np.stack([f128, sign(f128, 16), f64, sign(f64, 8), r * 0, r * 0, r * 0, r * 0], 1)
    three["e0"] = np.zeros((P, P))
    c3 = np.concatenate([np.asarray(three[n], f) for n, _ in C_3], 1)
    return c1, c3


def lora2(g):
    out = np.zeros((PAIRS + 1, P, 4, P), np.float32)
    for k, name in enumerate(("rwkv_w2_f", "rwkv_w2_b", "rwkv_a2_f", "rwkv_a2_b")):
        out[:PAIRS, :LORA, k, :] = g[name].reshape(LORA, PAIRS, P).transpose(1, 0, 2)
    return out.reshape(PAIRS + 1, P, 4 * P)


def kernel(**inputs):
    import concourse.bacc as _bacc
    from concourse.bass_utils import run_bass_kernel_spmd as _run

    g = {name: np.asarray(x) for name, x in inputs.items()}
    c1, c3 = constants()
    p1, p2, p3 = params(g)
    arrays = {
        "x": fm(g["x"][0]), "weights": weight_slots(g), "ada": ada_slots(g), "const1": c1, "const3": c3, "params1": p1, "params2": p2,
        "params3": p3, "lora2": lora2(g), "p": fm(g["p_2"][0, 0]), "b_rows": g["b_in_2"][:, 2 * WIDTH:],
        "positions": g["positions_3"].reshape(1, T),
    }
    nc = _bacc.Bacc("TRN2", target_bir_lowering=False, num_devices=1, dynamic_dma_scratch_size=1024)
    feeds, a = {}, {}
    for name, x in arrays.items():
        x = np.ascontiguousarray(x)
        feeds[f"in_{name}"] = x
        a[name] = nc.dram_tensor(f"in_{name}", x.shape, mybir.dt.from_np(x.dtype), kind="ExternalInput").ap()
    a["out"] = nc.dram_tensor("out", (P, DC, T), F32, kind="ExternalOutput").ap()
    build_program(nc, a)
    r = _run(nc, [feeds], core_ids=[0])
    return r.results[0]["out"].transpose(2, 1, 0).reshape(1, T, D)
```
